# Optimizing a Trainium2 kernel written in Bass

```python
import math
import jax
import jax.numpy as jnp
from jax import lax
import numpy as np

D_MODEL = 1024
BATCH = 1
SEQ = 512
DEPTH = 2

GRID_W = 64
CTX_LEN = 256
HEAD_DIM = 64
A_WIDTH = D_MODEL // 4
A_HEADS = A_WIDTH // HEAD_DIM
A_DECAY_LORA = 32
A_ICLR_LORA = 32
A_GATE_LORA = 64
B_WIDTH = D_MODEL // 2
B_V_DIM = 2 * HEAD_DIM
B_HEADS = B_WIDTH // B_V_DIM
Q_BLOCK = 128
ROPE_BASE = 10000.0
C_WIDTH = D_MODEL - A_WIDTH - B_WIDTH
C_HEADS = C_WIDTH // HEAD_DIM
C_CHUNK = 64
MIN_FORGET = 1e-30
PEER_HEADS = 8
PEER_NKEYS = 128
PEER_EXPERTS = PEER_NKEYS * PEER_NKEYS
PEER_QDIM = 256
PEER_TOPK = 16
PEER_TOKEN_BLOCK = 128
DEEPNORM_ALPHA = (2.0 * DEPTH) ** 0.25
DEEPNORM_BETA = (8.0 * DEPTH) ** -0.25
LN_EPS = 1e-5
RWKV_GN_EPS = 64e-5
IN_SPLITS = (A_WIDTH, A_WIDTH, A_WIDTH, A_DECAY_LORA, A_ICLR_LORA, A_GATE_LORA,
             2 * B_HEADS * HEAD_DIM, 2 * B_HEADS * HEAD_DIM, B_HEADS * B_V_DIM,
             C_WIDTH, C_WIDTH, C_WIDTH, C_WIDTH, C_WIDTH)
IN_WIDTH = sum(IN_SPLITS)

kernel_name = 'hybrid_rwkv7_diffattn_hgrn2_peer_dit'

def split_heads(t, n):
    return t.reshape(t.shape[:-1] + (n, t.shape[-1] // n))

def time_major(t):
    return jnp.swapaxes(t, 0, 1).astype(jnp.float32)

def layer_norm(x, w=None, b=None):
    xf = x.astype(jnp.float32)
    xc = xf - xf.mean(-1, keepdims=True)
    y = (xc * lax.rsqrt((xc * xc).mean(-1, keepdims=True) + LN_EPS)).astype(x.dtype)
    if w is not None:
        y = y * w + b
    return y

def rms_norm(x, w):
    xf = x.astype(jnp.float32)
    return (xf * lax.rsqrt((xf * xf).mean(-1, keepdims=True) + LN_EPS)).astype(x.dtype) * w

def modulate(x, shift, scale):
    return layer_norm(x) * (1.0 + scale) + shift

def split_cols(h):
    parts, start = [], 0
    for n in IN_SPLITS:
        parts.append(h[..., start:start + n])
        start += n
    return parts

def short_conv_centered(x, w):
    xp = jnp.pad(x, ((0, 0), (1, 1), (0, 0)))
    return w[0] * xp[:, :-2] + w[1] * xp[:, 1:-1] + w[2] * xp[:, 2:]

def axial_rope_tables(n_rows, dtype):
    row = jnp.repeat(jnp.arange(n_rows), GRID_W).astype(jnp.float32)
    col = jnp.tile(jnp.arange(GRID_W), n_rows).astype(jnp.float32)
    quarter = HEAD_DIM // 4
    inv_freq = ROPE_BASE ** (-2.0 * jnp.arange(quarter, dtype=jnp.float32) / (HEAD_DIM // 2))
    ang_r = row[:, None] * inv_freq
    ang_c = col[:, None] * inv_freq
    shape = (1, row.shape[0], 1, 1, quarter)
    return tuple(f(a).reshape(shape).astype(dtype) for a in (ang_r, ang_c) for f in (jnp.cos, jnp.sin))

def apply_axial_rope(t, rope):
    cr, sr, cc, sc = rope
    x1, x2, x3, x4 = jnp.split(t, 4, axis=-1)
    return jnp.concatenate([x1 * cr - x2 * sr, x2 * cr + x1 * sr,
                            x3 * cc - x4 * sc, x4 * cc + x3 * sc], axis=-1)

def bidirectional_scan(scan_fn, ctx_dirs, lat_dirs, s0):
    rev = lambda tup: tuple(jnp.flip(a, 0) for a in tup)
    s, oc_f = scan_fn(ctx_dirs[0], s0)
    _, ol_f = scan_fn(lat_dirs[0], s)
    s, oc_b = scan_fn(rev(ctx_dirs[1]), s0)
    _, ol_b = scan_fn(rev(lat_dirs[1]), s)
    return oc_f + jnp.flip(oc_b, 0), ol_f + jnp.flip(ol_b, 0)

def rwkv7_scan(inputs, s0):
    def step(S, xs):
        r, w, k, v, a, b = xs
        sa = jnp.einsum('bhvk,bhk->bhv', S, a)
        S = S * w[:, :, None, :] + sa[..., None] * b[:, :, None, :] + v[..., None] * k[:, :, None, :]
        return S, jnp.einsum('bhvk,bhk->bhv', S, r)
    return lax.scan(step, s0, inputs)

def rwkv7_prepare(r, k, v, w_lo, a_lo, g_lo, P):
    r, k, v = jnp.split(short_conv_centered(jnp.concatenate([r, k, v], -1), P['rwkv_conv']), 3, axis=-1)
    a = jax.nn.sigmoid(P['rwkv_a0'] + a_lo @ P['rwkv_a2'])
    g = jax.nn.sigmoid(g_lo) @ P['rwkv_g2']
    kk = split_heads(k * P['rwkv_k_k'], A_HEADS).astype(jnp.float32)
    kk = kk * lax.rsqrt(jnp.maximum(jnp.sum(kk * kk, -1, keepdims=True), 1e-24))
    k = k * (1.0 + (a - 1.0) * P['rwkv_k_a'])
    tw = jnp.tanh(w_lo)
    decays = []
    for d in range(2):
        wl = (P['rwkv_w0'][d] + tw @ P['rwkv_w2'][d]).astype(jnp.float32)
        decays.append(split_heads(jnp.exp(-jnp.exp(-jax.nn.softplus(-wl) - 0.5)), A_HEADS))
    return dict(r=split_heads(r, A_HEADS), k=split_heads(k, A_HEADS), v=split_heads(v, A_HEADS),
                kk=kk, a=split_heads(a, A_HEADS).astype(jnp.float32), decay=tuple(decays), g=g)

def rwkv7_scan_inputs(p):
    r, k, v = time_major(p['r']), time_major(p['k']), time_major(p['v'])
    a_vec = time_major(-p['kk'])
    b_vec = time_major(p['kk'] * p['a'])
    return tuple((r, time_major(dec), k, v, a_vec, b_vec) for dec in p['decay'])

def rwkv7_finish(o, p, P):
    o = jnp.swapaxes(o, 0, 1)
    oc = o - o.mean(-1, keepdims=True)
    y = oc * lax.rsqrt((oc * oc).mean(-1, keepdims=True) + RWKV_GN_EPS)
    bsz, t = y.shape[:2]
    y = y.reshape(bsz, t, A_WIDTH).astype(p['g'].dtype) * P['rwkv_ln_w'] + P['rwkv_ln_b']
    bonus = jnp.sum(p['r'] * p['k'] * split_heads(P['rwkv_r_k'], A_HEADS), -1, keepdims=True) * p['v']
    return (y + bonus.reshape(bsz, t, A_WIDTH)) * p['g']

def diff_softmax_attend(q, k, v, lam):
    s = jnp.einsum('bqhmd,bkhmd->bhmqk', q, k).astype(jnp.float32) * (HEAD_DIM ** -0.5)
    p = jax.nn.softmax(s, axis=-1)
    a = p[:, :, 0] - lam * p[:, :, 1]
    return jnp.einsum('bhqk,bkhe->bqhe', a.astype(v.dtype), v)

def diff_attention_mixer(q_c, k_c, v_c, q_l, k_l, v_l, rope, P, layer_idx, need_ctx):
    qk_heads = lambda t: t.reshape(t.shape[:2] + (B_HEADS, 2, HEAD_DIM))
    q_c, k_c, v_c = qk_heads(q_c), qk_heads(k_c), split_heads(v_c, B_HEADS)
    q_l = apply_axial_rope(qk_heads(q_l), rope)
    k_l = apply_axial_rope(qk_heads(k_l), rope)
    v_l = split_heads(v_l, B_HEADS)
    lam_init = 0.8 - 0.6 * math.exp(-0.3 * layer_idx)
    lq1, lk1, lq2, lk2 = P['diff_lambda'].astype(jnp.float32)
    lam = jnp.exp(jnp.sum(lq1 * lk1)) - jnp.exp(jnp.sum(lq2 * lk2)) + lam_init
    k_all = jnp.concatenate([k_l, k_c], axis=1)
    v_all = jnp.concatenate([v_l, v_c], axis=1)
    bsz, n_lat = q_l.shape[:2]
    n_blk = n_lat // Q_BLOCK
    q_blocks = jnp.moveaxis(q_l.reshape((bsz, n_blk, Q_BLOCK) + q_l.shape[2:]), 1, 0)
    o_blocks = lax.map(lambda qb: diff_softmax_attend(qb, k_all, v_all, lam), q_blocks)
    o_l = jnp.moveaxis(o_blocks, 0, 1).reshape(bsz, n_lat, B_HEADS, B_V_DIM)

    def finish(o):
        y = rms_norm(o, P['diff_subln_w']) * (1.0 - lam_init)
        return y.reshape(y.shape[:2] + (B_WIDTH,))

    y_l = finish(o_l)
    y_c = finish(diff_softmax_attend(q_c, k_c, v_c, lam)) if need_ctx else None
    return y_c, y_l

def hgrn2_chunk_scan(inputs, s0):
    q, k, logf, v = inputs
    n_tok = q.shape[0]
    n_chunk = n_tok // C_CHUNK
    causal = jnp.tril(jnp.ones((C_CHUNK, C_CHUNK), dtype=bool))[:, :, None, None, None]

    def step(S, xs):
        qc, kc, lf, vc = xs
        b = jnp.cumsum(lf, axis=0)
        inter = jnp.einsum('tbhd,bhde->tbhe', qc * jnp.exp(b), S)
        diff = b[:, None] - b[None, :]
        decay = jnp.where(causal, jnp.exp(jnp.where(causal, diff, 0.0)), 0.0)
        attn = jnp.einsum('tbhd,sbhd,tsbhd->bhts', qc, kc, decay)
        intra = jnp.einsum('bhts,sbhe->tbhe', attn, vc)
        b_last = b[-1]
        S = jnp.exp(b_last)[..., None] * S + jnp.einsum('sbhd,sbhe->bhde', kc * jnp.exp(b_last[None] - b), vc)
        return S, inter + intra

    chunked = tuple(a.reshape((n_chunk, C_CHUNK) + a.shape[1:]) for a in inputs)
    S, o = lax.scan(step, s0, chunked)
    return S, o.reshape((n_tok,) + o.shape[2:])

def hgrn2_prepare(q, zf_f, zf_b, i, g, lb):
    ks, logfs = [], []
    for z in (zf_f, zf_b):
        zf = z.astype(jnp.float32)
        f = lb + (1.0 - lb) * jax.nn.sigmoid(zf)
        logfs.append(split_heads(jnp.log(jnp.maximum(f, MIN_FORGET)), C_HEADS))
        ks.append(split_heads((1.0 - lb) * jax.nn.sigmoid(-zf), C_HEADS))
    return dict(q=split_heads(jax.nn.silu(q), C_HEADS), k=tuple(ks), logf=tuple(logfs),
                v=split_heads(i, C_HEADS), g=g)

def hgrn2_scan_inputs(p):
    q, v = time_major(p['q']), time_major(p['v'])
    return tuple((q, time_major(k), time_major(lf), v) for k, lf in zip(p['k'], p['logf']))

def hgrn2_finish(o, p, P):
    o = jnp.swapaxes(o, 0, 1)
    g = split_heads(p['g'], C_HEADS)
    y = rms_norm(o, P['hgrn_norm_w']).astype(g.dtype) * jax.nn.silu(g)
    return y.reshape(y.shape[:2] + (C_WIDTH,))

def token_mixers(h_ctx, h_lat, P, layer_idx, lb, rope, need_ctx):
    pc, pl = split_cols(h_ctx), split_cols(h_lat)
    bsz = h_lat.shape[0]
    ac, al = rwkv7_prepare(*pc[0:6], P), rwkv7_prepare(*pl[0:6], P)
    s0a = jnp.zeros((bsz, A_HEADS, HEAD_DIM, HEAD_DIM), jnp.float32)
    oa_c, oa_l = bidirectional_scan(rwkv7_scan, rwkv7_scan_inputs(ac), rwkv7_scan_inputs(al), s0a)
    ya_l = rwkv7_finish(oa_l, al, P)
    yb_c, yb_l = diff_attention_mixer(*pc[6:9], *pl[6:9], rope, P, layer_idx, need_ctx)
    cc, cl = hgrn2_prepare(*pc[9:14], lb), hgrn2_prepare(*pl[9:14], lb)
    s0c = jnp.zeros((bsz, C_HEADS, HEAD_DIM, HEAD_DIM), jnp.float32)
    oc_c, oc_l = bidirectional_scan(hgrn2_chunk_scan, hgrn2_scan_inputs(cc), hgrn2_scan_inputs(cl), s0c)
    yc_l = hgrn2_finish(oc_l, cl, P)
    y_lat = jnp.concatenate([ya_l, yb_l, yc_l], axis=-1)
    y_ctx = None
    if need_ctx:
        y_ctx = jnp.concatenate([rwkv7_finish(oa_c, ac, P), yb_c, hgrn2_finish(oc_c, cc, P)], axis=-1)
    return y_ctx, y_lat

def peer_ffn(u, P):
    shp = u.shape
    n_tok = shp[0] * shp[1]
    ut = u.reshape(n_tok // PEER_TOKEN_BLOCK, PEER_TOKEN_BLOCK, shp[-1])

    def block(ub):
        t = ub.shape[0]
        q = (ub @ P['peer_wq']).reshape(t, PEER_HEADS, 2, PEER_QDIM // 2)
        s = jnp.einsum('thpd,pkd->thpk', q, P['peer_subkeys']).astype(jnp.float32)
        sv, si = lax.top_k(s, PEER_TOPK)
        cand = (sv[:, :, 0, :, None] + sv[:, :, 1, None, :]).reshape(t, PEER_HEADS, PEER_TOPK * PEER_TOPK)
        top, ci = lax.top_k(cand, PEER_TOPK)
        e = (jnp.take_along_axis(si[:, :, 0], ci // PEER_TOPK, axis=-1) * PEER_NKEYS
             + jnp.take_along_axis(si[:, :, 1], ci % PEER_TOPK, axis=-1))
        gate = jax.nn.softmax(top, axis=-1)
        e = e.reshape(t, PEER_HEADS * PEER_TOPK)
        gate = gate.reshape(t, PEER_HEADS * PEER_TOPK)
        act = jax.nn.gelu(jnp.einsum('tkd,td->tk', P['peer_u'][e], ub).astype(jnp.float32), approximate=False)
        return jnp.einsum('tk,tkd->td', (gate * act).astype(ub.dtype), P['peer_v'][e])

    return lax.map(block, ut).reshape(shp)

def setup_inputs(seed: int = 0) -> dict:
    key = jax.random.key(seed)
    ks = iter(jax.random.split(key, 40))
    f32 = jnp.float32
    nrm = lambda shape, scale=1.0: jax.random.normal(next(ks), shape, f32) * scale
    L, D = DEPTH, D_MODEL
    conv_center = jnp.array([0.0, 1.0, 0.0], f32)[None, :, None]
    return {
        'x': nrm((BATCH, SEQ, D)),
        'c': nrm((BATCH, D)),
        'ctx': nrm((BATCH, CTX_LEN, D)),
        'c_ctx': nrm((D,)),
        'ada_w': nrm((L, D, 6 * D), D ** -0.5),
        'ada_b': nrm((L, 6 * D), 0.01),
        'w_in': nrm((L, D, IN_WIDTH), D ** -0.5),
        'rwkv_conv': conv_center + nrm((L, 3, 3 * A_WIDTH), 0.1),
        'rwkv_w0': jnp.linspace(-6.0, -1.0, A_WIDTH, dtype=f32) + nrm((L, 2, A_WIDTH), 0.1),
        'rwkv_w2': nrm((L, 2, A_DECAY_LORA, A_WIDTH), 0.1),
        'rwkv_a0': nrm((L, A_WIDTH), 0.1),
        'rwkv_a2': nrm((L, A_ICLR_LORA, A_WIDTH), 0.1),
        'rwkv_g2': nrm((L, A_GATE_LORA, A_WIDTH), 2.0 * A_GATE_LORA ** -0.5),
        'rwkv_k_k': 0.85 + nrm((L, A_WIDTH), 0.05),
        'rwkv_k_a': 1.0 + nrm((L, A_WIDTH), 0.05),
        'rwkv_r_k': nrm((L, A_WIDTH), 0.1),
        'rwkv_ln_w': 1.0 + nrm((L, A_WIDTH), 0.05),
        'rwkv_ln_b': nrm((L, A_WIDTH), 0.01),
        'diff_lambda': nrm((L, 4, HEAD_DIM), 0.1),
        'diff_subln_w': 1.0 + nrm((L, B_V_DIM), 0.05),
        'hgrn_lb_logits': 1.0 + nrm((L, C_WIDTH), 0.1),
        'hgrn_norm_w': 1.0 + nrm((L, HEAD_DIM), 0.05),
        'w_out': nrm((L, D, D), DEEPNORM_BETA * D ** -0.5),
        'ln1_w': 1.0 + nrm((L, D), 0.05),
        'ln1_b': nrm((L, D), 0.01),
        'peer_wq': nrm((L, D, PEER_HEADS * PEER_QDIM), D ** -0.5),
        'peer_subkeys': nrm((L, 2, PEER_NKEYS, PEER_QDIM // 2), (PEER_QDIM // 2) ** -0.5),
        'peer_u': nrm((L, PEER_EXPERTS, D), D ** -0.5),
        'peer_v': nrm((L, PEER_EXPERTS, D), DEEPNORM_BETA),
        'ln2_w': 1.0 + nrm((L, D), 0.05),
        'ln2_b': nrm((L, D), 0.01),
    }

def reference(x, c, ctx, c_ctx, ada_w, ada_b, w_in, rwkv_conv, rwkv_w0, rwkv_w2, rwkv_a0, rwkv_a2,
              rwkv_g2, rwkv_k_k, rwkv_k_a, rwkv_r_k, rwkv_ln_w, rwkv_ln_b, diff_lambda, diff_subln_w,
              hgrn_lb_logits, hgrn_norm_w, w_out, ln1_w, ln1_b, peer_wq, peer_subkeys, peer_u, peer_v,
              ln2_w, ln2_b):
    n_rows = x.shape[1] // GRID_W
    rope = axial_rope_tables(n_rows, x.dtype)
    lb_p = jax.nn.softmax(hgrn_lb_logits.astype(jnp.float32), axis=0)
    lower_bounds = jnp.cumsum(lb_p, axis=0) - lb_p[0]
    xc = ctx
    for l in range(DEPTH):
        last = l == DEPTH - 1
        P = dict(rwkv_conv=rwkv_conv[l], rwkv_w0=rwkv_w0[l], rwkv_w2=rwkv_w2[l], rwkv_a0=rwkv_a0[l],
                 rwkv_a2=rwkv_a2[l], rwkv_g2=rwkv_g2[l], rwkv_k_k=rwkv_k_k[l], rwkv_k_a=rwkv_k_a[l],
                 rwkv_r_k=rwkv_r_k[l], rwkv_ln_w=rwkv_ln_w[l], rwkv_ln_b=rwkv_ln_b[l],
                 diff_lambda=diff_lambda[l], diff_subln_w=diff_subln_w[l], hgrn_norm_w=hgrn_norm_w[l],
                 peer_wq=peer_wq[l], peer_subkeys=peer_subkeys[l], peer_u=peer_u[l], peer_v=peer_v[l])
        m_lat = (jax.nn.silu(c) @ ada_w[l] + ada_b[l])[:, None, :]
        m_ctx = jax.nn.silu(c_ctx) @ ada_w[l] + ada_b[l]
        sh1, sc1, g1, sh2, sc2, g2 = jnp.split(m_lat, 6, axis=-1)
        ch1, cs1, cg1, ch2, cs2, cg2 = jnp.split(m_ctx, 6, axis=-1)
        u_lat = modulate(x, sh1, sc1)
        u_ctx = modulate(xc, ch1, cs1)
        y_ctx, y_lat = token_mixers(u_ctx @ w_in[l], u_lat @ w_in[l], P, l, lower_bounds[l], rope, not last)
        x = layer_norm(DEEPNORM_ALPHA * x + g1 * (y_lat @ w_out[l]), ln1_w[l], ln1_b[l])
        x = layer_norm(DEEPNORM_ALPHA * x + g2 * peer_ffn(modulate(x, sh2, sc2), P), ln2_w[l], ln2_b[l])
        if not last:
            xc = layer_norm(DEEPNORM_ALPHA * xc + cg1 * (y_ctx @ w_out[l]), ln1_w[l], ln1_b[l])
            xc = layer_norm(DEEPNORM_ALPHA * xc + cg2 * peer_ffn(modulate(xc, ch2, cs2), P), ln2_w[l], ln2_b[l])
    return x


_drawn_inputs = setup_inputs


def setup_inputs(seed=0):
    import zlib

    import numpy as np

    out = dict(_drawn_inputs(seed))
    spreads = {}
    factors = {'rwkv_ln_w': 2.699,
     'rwkv_ln_b': 7.3,
     'diff_subln_w': 2.809,
     'hgrn_lb_logits': 23.914,
     'hgrn_norm_w': 3.103,
     'ln2_b': 2.816}
    for name, (base, spread) in spreads.items():
        noise = np.random.default_rng([zlib.crc32(name.encode()), seed]).standard_normal(out[name].shape)
        drawn = base * np.exp(spread * noise) if base else spread * noise
        out[name] = jnp.asarray(drawn.astype(out[name].dtype))
    for name, factor in factors.items():
        out[name] = (out[name] * factor).astype(out[name].dtype)
    return out
```

```python
import math
from contextlib import ExitStack

import numpy as np
import concourse.bass as bass
from concourse import mybir
from concourse.bass import IndirectOffsetOnAxis

ALU = mybir.AluOpType
ACT = mybir.ActivationFunctionType
AX = mybir.AxisListType
F32 = mybir.dt.float32
U32 = mybir.dt.uint32
I32 = mybir.dt.int32
U8 = mybir.dt.uint8

P = 128
DEPTH, D, SEQ, CTX = 2, 1024, 512, 256
KB = D // P
T = CTX + SEQ
NT = T // P
CT = CTX // P
GRID_W, HD = 64, 64
BH = 4
LEVELS = 7
HEADS, NKEYS, TOPK = 8, 128, 16
EXPERTS = NKEYS * NKEYS
ALPHA = (2.0 * DEPTH) ** 0.25
EPS, GN_EPS, MIN_FORGET = 1e-5, 64e-5, 1e-30
LN_SHIFT = 50
SCALE = HD ** -0.5
SLOTS = 4
PIECE = 1024
GSLOTS = 8
GROUP = 4
ITER = HEADS * TOPK // (2 * GROUP)
GSTEP = 2 * GROUP + 1
ARENA = 24500
ADA, RW, AQK, AV, HF, HT, WO, WQ = 48, 7, 8, 4, 6, 4, 8, 16
PIECES = ADA + RW + AQK + AV + HF + HT + WO + WQ
C_CONV, C_A0, C_W0, C_KK, C_KA, C_RK, C_ADAB = 0, 18, 20, 24, 26, 28, 30
NCOL = C_ADAB + 48
R_GNW, R_GNB, R_SUB, R_HN, R_LAM = 0, 256, 512, 640, 704
NROW = 960
K_ID, K_ROT, K_ONES, K_BD, K_COS, K_SIN, K_IOTA = 0, 128, 256, 384, 512, 1024, 1536
K_HSEL, K_HALF, K_INV = 1552, 1554, 1556
NCF = K_INV + 2 * LEVELS * P
B_LEV, B_DIAG, B_STRICT, B_INCL = 0, 2 * LEVELS, 2 * LEVELS + 1, 2 * LEVELS + 3
NCB = B_INCL + 2


def orders():
    return [list(range(NT)), list(range(CT))[::-1] + list(range(CT, NT))[::-1]]


class Steps:

    def __init__(self, eng, sem, marks, chained):
        self.eng, self.sem, self.marks, self.chained, self.n = eng, sem, marks, chained, 0

    def __call__(self, ins, *name):
        self.n += 1
        ins.then_inc(self.sem, 1)
        if name:
            self.marks[name] = (self.sem.name, self.n)
        if self.chained:
            self.eng.wait_ge(self.sem, self.n)


def build(nc, a, marks):
    with ExitStack() as ctx:
        def sb(name, n, dt=F32):
            return ctx.enter_context(nc.sbuf_tensor(name, [P, n], dt))

        def sem(name):
            return ctx.enter_context(nc.semaphore(name))

        X = sb("x_tokens", NT * D)
        XT = sb("u_features", KB * T)
        YT = sb("y_features", KB * T)
        CF = sb("consts", NCF)
        CBW = sb("masks", NCB * P // 4, U32)
        CB = CBW[:].bitcast(U8)
        COL = sb("param_cols", NCOL)
        ROW = sb("param_rows", NROW)
        SW = sb("lora_weights", 512)
        SK = sb("subkeys", 2 * NKEYS)
        WR = sb("weight_ring", SLOTS * PIECE)
        MC = sb("mod_cols", 96)
        CC = sb("cond_cols", 2 * KB)
        ST = sb("stats", 64)
        LAM = sb("lambda", 4)
        LB = sb("lower_bounds", 16)
        AR = sb("arena", ARENA)
        PS = ctx.enter_context(nc.psum_tensor("psum", [P, 4096], F32))

        names = ["tensor_steps", "vector_steps", "scalar_steps", "pool_steps", "piece_used", "consts_loaded",
                 "params_loaded", "x_loaded", "ln_rows_loaded", "stored", "ids_staged", "expert_steps", "gelu_done"]
        SEM = {n: sem(n) for n in names}
        piece_in = [sem(f"piece_in{i}") for i in range(SLOTS)]
        rows_in = [sem(f"rows_in{i}") for i in range(GSLOTS)]

        def at(*name):
            if "real" in marks and name not in marks:
                raise KeyError(name)
            s, n = marks.get(name, ("vector_steps", 1))
            return SEM[s], n

        def bank(b, lo=0, hi=512):
            return PS[:, 512 * b + lo:512 * b + hi]

        def cf(k, n=P):
            return CF[:, k:k + n]

        def mask(i):
            return CB[:, i * P:(i + 1) * P]

        def x_tile(t):
            return X[:, t * D:(t + 1) * D]

        def xt(k, lo=0, hi=T):
            return XT[:, k * T + lo:k * T + hi]

        def yt(k, lo=0, hi=T):
            return YT[:, k * T + lo:k * T + hi]

        def turned(b, t):
            return PS[:, 512 * b + 256 + t * P:512 * b + 256 + (t + 1) * P]

        def rep(ap, n):
            return ap.unsqueeze(1).broadcast_to([P, n, ap.shape[-1]])

        def spread(ap, n):
            return ap.unsqueeze(2).broadcast_to([P, ap.shape[-1], n])

        def split(ap, n):
            return ap.rearrange("p (n c) -> p n c", n=n)

        def runs(ap, lev, second):
            return ap.rearrange("p (n two m) -> p n two m", two=2, m=1 << lev)[:, :, second, :]

        def parity_heads(ap):
            return ap.rearrange("p (n two c) -> p two n c", n=2, two=2)

        def parity_banks(b, c):
            return PS[:, 512 * b:512 * b + 1024].rearrange("p (two n) -> p two n", two=2)[:, :, c:c + 256]\
                .rearrange("p two (n c) -> p two n c", n=2)

        def rep4(ap):
            return ap.unsqueeze(1).unsqueeze(1).broadcast_to([P, 2, 2, ap.shape[-1]])

        def tiles(l):
            return list(range(NT)) if l + 1 < DEPTH else list(range(CT, NT))

        ident = cf(K_ID)
        top = [0]

        def take(n):
            v = AR[:, top[0]:top[0] + n]
            top[0] += n
            assert top[0] <= ARENA, top[0]
            return v

        XN = take(NT * D)
        SQ = take(D)
        BC = [take(D) for _ in range(4)]
        LNR = [take(D) for _ in range(2)]
        MR = [take(512)[0:2, :] for _ in range(2)]
        top[0] = 0
        RAW = take(7 * T)
        CV = take(6 * T)
        r_, k_, v_ = (CV[:, n * 2 * T:(n + 1) * 2 * T] for n in range(3))
        nkk, bv, lw0 = (RAW[:, n * 2 * T:(n + 1) * 2 * T] for n in range(3))
        lo_ = RAW[:, 6 * T:7 * T]
        lw1 = YT[:, 6 * T:8 * T]
        RA = YT[:, 2 * T:4 * T]
        VTM = YT[:, 4 * T:6 * T]
        BON = take(24)
        RM = take(48)
        RO = v_
        lw_ = [lw0, lw1]
        rsets = [{n: take(m) for n, m in dict(b=256, ta=256, tr=256, tb=256, tk=256, tm=768, abT=512, akT=512, qbT=512,
                                              qkT=512, T=512, G=512, X=512, x2=256, w=256, u=256, s=256, sm=256,
                                              bt=2, mc=2, em=2).items()} for d in range(2)]
        top[0] = 0
        QA, KA = take(4 * T), take(4 * T)
        VA = take(NT * 512)
        RT = take(SEQ)
        PA = [[take(T) for _ in range(2)] for _ in range(2)]
        PT_ = [take(T) for _ in range(2)]
        OA = take(NT * 512)
        OS = take(NT * 512)
        AST = take(64)
        top[0] = 0
        HQ = take(2 * T)
        HZ = [take(2 * T) for _ in range(2)]
        HK = [take(2 * T) for _ in range(2)]
        HS = take(2 * T)
        HI, HG, HO = take(2 * T), take(2 * T), take(2 * T)
        HM = take(24)
        hsets = [{n: take(m) for n, m in dict(b=256, eb=256, qh=256, kh=256, ktm=256, dd=LEVELS * 256, at=512,
                                              s=256, s1=256, bl=2, el=2).items()} for d in range(2)]
        top[0] = 0
        QT = take(16 * T)
        SC = take(2048)
        CAND = take(2048)
        OH = take(2048)
        SV, SIF = take(256), take(256)
        SI = take(256).bitcast(U32)
        TOP = take(P)
        CI = take(P).bitcast(U32)
        CIJ = take(2 * P).bitcast(U32)
        CF2 = take(2 * P)
        E0 = take(2 * P)
        GS = take(16)
        GATE = take(NT * P)
        IDX = take(NT * P).bitcast(U32)
        U2 = YT
        GB = [XT[:, i * 2048:(i + 1) * 2048] for i in range(3)] + [AR[:, i * 2048:(i + 1) * 2048] for i in range(5)]
        ACC = AR[:, 5 * 2048:5 * 2048 + D]
        assert 5 * 2048 + D <= 16 * T
        JUNK = SC[:, 0:D]
        G2 = [CAND[:, 0:D], SC[:, D:2 * D]]
        LNR2 = [CAND[:, D:2 * D], OH[:, 0:D]]
        SQ2 = OH[:, D:2 * D]
        DOT, GEL, WGT = SV[:, 0:8], SV[:, 16:24], SV[:, 32:40]
        IDS = SIF[:, 0:8].bitcast(U32)
        DUM = SIF[:, 16:17]

        block = ctx.enter_context(nc.Block())

        @block.sync
        def _(sp):
            sp.dma_start(CF[:], a["cf"]).then_inc(SEM["consts_loaded"], 16)
            sp.dma_start(CBW[:], a["cb"]).then_inc(SEM["consts_loaded"], 16)
            sp.dma_start(CC[:], a["cc"]).then_inc(SEM["consts_loaded"], 16)
            xv = X[:].rearrange("p (t n) -> p t n", t=NT)
            sp.dma_start(xv[:, 0:CT, :], a["ctx"].rearrange("b (t p) n -> p (b t) n", p=P)).then_inc(SEM["x_loaded"], 16)
            sp.dma_start(xv[:, CT:NT, :], a["x"].rearrange("b (t p) n -> p (b t) n", p=P)).then_inc(SEM["x_loaded"], 16)
            total = DEPTH * PIECES
            for j in range(SLOTS):
                sp.dma_start(WR[:, j * PIECE:(j + 1) * PIECE], a["ws"][j]).then_inc(piece_in[j], 16)
            with sp.Fori(1, total // SLOTS) as i:
                for j in range(SLOTS):
                    sp.wait_ge(SEM["piece_used"], i * SLOTS + (j + 1 - SLOTS))
                    sp.dma_start(WR[:, j * PIECE:(j + 1) * PIECE],
                                 a["ws"][bass.ds(i * SLOTS + j, 1)].rearrange("a p n -> p (a n)")).then_inc(piece_in[j], 16)
            for n in range(total // SLOTS * SLOTS, total):
                j = n % SLOTS
                sp.wait_ge(SEM["piece_used"], n + 1 - SLOTS)
                sp.dma_start(WR[:, j * PIECE:(j + 1) * PIECE], a["ws"][n]).then_inc(piece_in[j], 16)
            sp.wait_ge(*at("final", DEPTH - 1, NT - 1))
            sp.dma_start(a["out"].rearrange("b (t p) n -> p (b t) n", p=P), xv[:, CT:NT, :]).then_inc(SEM["stored"], 16)
            sp.wait_ge(SEM["stored"], 16)

        @block.tensor
        def _(pe):
            done = Steps(pe, SEM["tensor_steps"], marks, False)
            piece = [0]

            def mm(o, w, x, first=True, last=True):
                return pe.matmul(o, w, x, start=first, stop=last, skip_group_check=True)

            def piece_ready():
                n = piece[0]
                pe.wait_ge(piece_in[n % SLOTS], 16 * (n // SLOTS + 1))
                return WR[:, (n % SLOTS) * PIECE:(n % SLOTS + 1) * PIECE]

            def piece_done(ins, *name):
                piece[0] += 1
                ins.then_inc(SEM["piece_used"], 1)
                if name:
                    marks[name] = ("piece_used", piece[0])

            def project(l, what, count):
                for c in range(count):
                    w = piece_ready()
                    if c >= 2:
                        pe.wait_ge(*at(what + " copied", l, c - 2))
                    p0 = 2 * (c % 2)
                    for o, lo, hi in ((bank(p0, 256, 512), 0, CTX), (bank(p0 + 1), CTX, T)):
                        for k in range(KB):
                            ins = mm(o, w[:, k * P:(k + 1) * P], xt(k, lo, hi), k == 0, k == KB - 1)
                    piece_done(ins, what + " projected", l, c)

            def project_tokens(what, src, ts, *name):
                for c in range(KB // 2):
                    w = piece_ready()
                    for n, t in enumerate(ts):
                        for k in range(2):
                            ins = mm(bank(n), src(2 * c + k, t * P, (t + 1) * P), w[:, k * 512:(k + 1) * 512],
                                     c == 0 and k == 0, c == KB // 2 - 1 and k == 1)
                    piece_done(ins, *(name if c == KB // 2 - 1 else ()))

            def transpose_x(l, what, ts):
                for k in range(KB):
                    if k >= 3:
                        pe.wait_ge(*at(what + " modulated", l, k - 3))
                    for t in ts:
                        if k == 0:
                            pe.wait_ge(*at(what + " normed", l, t))
                        ins = pe.transpose(turned(2 * (k % 3), t), XN[:, t * D + k * P:t * D + (k + 1) * P], ident)
                    done(ins, what + " turned", l, k)

            def broadcast(l, what, firsts, streams):
                for n, s in enumerate(streams):
                    if n:
                        pe.wait_ge(*at(what + " kept", l, streams[0]))
                    for v, first in enumerate(firsts):
                        for k in range(KB):
                            j = 2 * (first + k) + s
                            ins = mm(bank(2 * v + k // 4, (k % 4) * P, (k % 4 + 1) * P),
                                     MC[:, j:j + 1].broadcast_to([P, P]), ident)
                    done(ins, what + " rows", l, s)

            def by_parity(b, h, c):
                return bank(b + h % 2, c + h // 2 * P, c + (h // 2 + 1) * P)

            def head_rows(h):
                return slice(64 * (h % 2), 64 * (h % 2) + 64)

            def block_cols(h):
                return slice((h // 2) * P, (h // 2 + 1) * P)

            pe.wait_ge(SEM["consts_loaded"], 48)
            for l in range(DEPTH):
                streams = [0, 1] if l + 1 < DEPTH else [0]
                if l == 0:
                    pe.wait_ge(*at("cond silu"))
                else:
                    pe.wait_ge(*at("final", l - 1, NT - 1))
                for c in range(ADA // 4 + 1):
                    if c < ADA // 4:
                        if c >= 2:
                            pe.wait_ge(*at("ada rows kept", l, c - 2))
                        for n in range(4):
                            w = piece_ready()
                            for j in range(2):
                                k = 2 * n + j
                                ins = mm(bank(5 + 2 * (c % 2))[0:2, :], CC[:, 2 * k:2 * k + 2], w[:, j * 512:(j + 1) * 512],
                                         k == 0, k == KB - 1)
                            piece_done(ins, "ada rows", l, c)
                    if c:
                        pe.wait_ge(*at("ada rows kept", l, c - 1))
                        for j in range(4):
                            n = 4 * (c - 1) + j
                            ins = mm(bank(6, 2 * n, 2 * n + 2), MR[(c - 1) % 2][:, j * P:(j + 1) * P], ident[0:2, 0:2])
                        done(ins, "ada turned", l, c - 1)
                transpose_x(l, "ln1", range(NT))
                pe.wait_ge(*at("ln1 modulated", l, KB - 1))
                project(l, "rwkv", RW)
                pe.wait_ge(*at("rwkv kk squared", l))
                for b in range(2):
                    pe.wait_ge(*at("rwkv copied", l, RW - 1))
                    mm(bank(2 * b, 256, 512), cf(K_BD), bv[:, b * T:b * T + CTX])
                    done(mm(bank(2 * b + 1), cf(K_BD), bv[:, b * T + CTX:(b + 1) * T]), "rwkv kk norm", l, b)
                pe.wait_ge(*at("rwkv lora in", l))
                for j in range(6):
                    rows = slice(32, 64) if j < 2 else slice(0, 32)
                    c0 = 256 if j >= 4 else 0
                    if j < 2:
                        pe.wait_ge(*at("rwkv kk floored", l, j))
                    if j >= 3:
                        pe.wait_ge(*at("rwkv gate read", l, j - 3))
                    w = SW[rows, c0 + (j % 2) * P:c0 + (j % 2 + 1) * P]
                    mm(bank(2 * (j % 3), 256, 512), w, lo_[rows, 0:CTX])
                    done(mm(bank(2 * (j % 3) + 1), w, lo_[rows, CTX:T]), "rwkv gate", l, j)
                for j in (3, 4, 5):
                    pe.wait_ge(*at("rwkv gate read", l, j))
                for t in range(NT):
                    for b in range(2):
                        c = t * 256 + b * P
                        ins = pe.transpose(PS[:, c:c + P], v_[:, b * T + t * P:b * T + (t + 1) * P], ident)
                done(ins, "rwkv v turned", l)
                pe.wait_ge(*at("rwkv gate read", l, 5))
                pe.wait_ge(*at("rwkv rk", l))
                for t in range(NT):
                    for b in range(2):
                        ins = mm(bank(7, t * 4 + 2 * b, t * 4 + 2 * b + 2), RA[:, b * T + t * P:b * T + (t + 1) * P],
                                 cf(K_HSEL, 2))
                done(ins, "rwkv bonus", l)
                pe.wait_ge(*at("rwkv ready", l))
                pe.wait_ge(*at("rwkv v kept", l))
                for i in range(NT):
                    R = [(d, orders()[d][i], rsets[d], 4 * d) for d in range(2)]
                    for d, t, q, b0 in R:
                        if i:
                            pe.wait_ge(*at("rwkv state", l, i - 1, d))
                        pe.wait_ge(*at("rwkv scaled", l, i, d))
                        for n, src in enumerate(("ta", "tb", "tk")):
                            for b in range(2):
                                c = 512 * b0 + (2 * n + b) * P
                                ins = pe.transpose(PS[:, c:c + P], q[src][:, b * P:(b + 1) * P], ident)
                        done(ins, "rwkv abk turned", l, i, d)
                    for d, t, q, b0 in R:
                        pe.wait_ge(*at("rwkv abk kept", l, i, d))
                        for n, (s, m) in enumerate((("tb", "ta"), ("tk", "ta"), ("tb", "tr"), ("tk", "tr"))):
                            for h in range(4):
                                ins = mm(by_parity(b0 + n // 2 * 2, h, n % 2 * 256), q[s][head_rows(h), block_cols(h)],
                                         q[m][head_rows(h), block_cols(h)])
                            done(ins, "rwkv scores", l, i, d, n)
                    for lev in range(LEVELS):
                        for d, t, q, b0 in R:
                            if lev == 0:
                                pe.wait_ge(*at("rwkv scores kept", l, i, d))
                            else:
                                pe.wait_ge(*at("rwkv T", l, i, d, lev - 1))
                            for h in range(4):
                                c = slice(h * P, (h + 1) * P)
                                if lev == 0:
                                    ins = mm(by_parity(b0, h, 0), q["ta"][head_rows(h), block_cols(h)],
                                             q["tb"][head_rows(h), block_cols(h)])
                                else:
                                    ins = mm(bank(b0, h * P, (h + 1) * P), q["abT"][:, c], q["T"][:, c])
                            done(ins, "rwkv AT", l, i, d, lev)
                        for d, t, q, b0 in R:
                            pe.wait_ge(*at("rwkv X", l, i, d, lev))
                            left, right = (0, 1) if d == 0 else (1, 0)
                            for h in range(4):
                                c = slice(h * P, (h + 1) * P)
                                G = ident if lev == 0 else q["G"][:, c]
                                if lev < LEVELS - 1:
                                    mm(runs(bank(b0 + 1, h * P, (h + 1) * P), lev, left), G, runs(q["X"][:, c], lev, left))
                                ins = mm(runs(bank(b0 + 2, h * P, (h + 1) * P), lev, right), q["X"][:, c],
                                         runs(G, lev, right))
                            done(ins, "rwkv dT", l, i, d, lev)
                    for d, t, q, b0 in R:
                        pe.wait_ge(*at("rwkv G", l, i, d, LEVELS - 1))
                        for h in range(4):
                            mm(bank(b0 + 3, h * 64, h * 64 + 64), q["akT"][:, h * P:(h + 1) * P],
                               VTM[:, t * 256 + h * 64:t * 256 + h * 64 + 64])
                            c = 512 * b0 + (h // 2) * P
                            ins = mm(PS[head_rows(h), c:c + P], q["tm"][:, h * 64:h * 64 + 64], q["G"][:, h * P:(h + 1) * P])
                        done(ins, "rwkv W", l, i, d)
                    for d, t, q, b0 in R:
                        pe.wait_ge(*at("rwkv W kept", l, i, d))
                        for b in range(2):
                            mm(bank(b0 + 1, b * P, (b + 1) * P), q["w"][:, b * P:(b + 1) * P],
                               q["sm"][:, b * P:(b + 1) * P], True, False)
                            for h in (2 * b, 2 * b + 1):
                                ins = mm(bank(b0 + 1, h * 64, h * 64 + 64), q["G"][:, h * P:(h + 1) * P],
                                         q["x2"][:, h * 64:h * 64 + 64], False, True)
                        done(ins, "rwkv U", l, i, d)
                    for d, t, q, b0 in R:
                        pe.wait_ge(*at("rwkv U kept", l, i, d))
                        for b in range(2):
                            c = slice(b * P, (b + 1) * P)
                            o = bank(b0 + 3, 256 + b * P, 256 + (b + 1) * P)
                            mm(o, q["tm"][:, 256 + b * P:256 + (b + 1) * P], q["u"][:, c], True, False)
                            mm(o, q["tm"][:, 512 + b * P:512 + (b + 1) * P],
                               VTM[:, t * 256 + b * P:t * 256 + (b + 1) * P], False, True)
                        for b in range(2):
                            c = slice(b * P, (b + 1) * P)
                            mm(bank(b0 + 2, b * P, (b + 1) * P), q["tr"][:, c], q["sm"][:, c], True, False)
                            for h in (2 * b, 2 * b + 1):
                                o = bank(b0 + 2, h * 64, h * 64 + 64)
                                mm(o, q["qbT"][:, h * P:(h + 1) * P], q["u"][:, h * 64:h * 64 + 64], False, False)
                                ins = mm(o, q["qkT"][:, h * P:(h + 1) * P],
                                         VTM[:, t * 256 + h * 64:t * 256 + h * 64 + 64], False, True)
                        done(ins, "rwkv out", l, i, d)
                for d in range(2):
                    pe.wait_ge(*at("rwkv state", l, NT - 1, d))
                for t in range(NT):
                    ins = mm(PS[:, t * 256:(t + 1) * 256], lo_[64:128, t * P:(t + 1) * P], SW[64:128, 0:256])
                done(ins, "rwkv g", l)
                pe.wait_ge(*at("rwkv y", l))
                for b in range(2):
                    for t in tiles(l):
                        ins = pe.transpose(turned(2 * b, t), RO[:, t * 256 + b * P:t * 256 + (b + 1) * P], ident)
                done(ins, "rwkv y turned", l)
                pe.wait_ge(*at("rwkv y features", l))
                project(l, "attn", AQK)
                pe.wait_ge(*at("attn copied", l, AQK - 1))
                project_tokens("attn", xt, range(NT), "attn v", l)
                for n in range(8):
                    if n >= 2:
                        pe.wait_ge(*at("rope", l, n - 2))
                    src = QA if n < 4 else KA
                    done(mm(bank(6 + n % 2), cf(K_ROT), src[:, (n % 4) * T + CTX:(n % 4 + 1) * T]), "rotated", l, n)
                pe.wait_ge(*at("rope", l, 7))
                pe.wait_ge(*at("attn v kept", l))
                jobs = [(t, h) for t in tiles(l) for h in range(BH)]
                for n in range(len(jobs) + 2):
                    if n < len(jobs):
                        t, h = jobs[n]
                        for m in range(2):
                            if n:
                                pe.wait_ge(*at("attn exp", l, n - 1, m))
                            rows = slice(64 * m, 64 * m + 64)
                            q = QA[rows, h * T + t * P:h * T + (t + 1) * P]
                            ins = mm(bank(2 * m, 256, 512), q, KA[rows, h * T:h * T + CTX])
                            if t >= CT:
                                ins = mm(bank(2 * m + 1), q, KA[rows, h * T + CTX:(h + 1) * T])
                            done(ins, "attn scores", l, n, m)
                    if 1 <= n <= len(jobs):
                        j = n - 1
                        nk = NT if jobs[j][0] >= CT else CT
                        pe.wait_ge(*at("attn a", l, j))
                        if j:
                            pe.wait_ge(*at("attn aT", l, j - 1))
                        for k in range(nk):
                            ins = pe.transpose(PS[:, 2048 + k * P:2048 + (k + 1) * P], PA[j % 2][0][:, k * P:(k + 1) * P], ident)
                        done(ins, "attn a turned", l, j)
                    if n >= 2:
                        j = n - 2
                        t, h = jobs[j]
                        nk = NT if t >= CT else CT
                        pe.wait_ge(*at("attn aT", l, j))
                        if j:
                            pe.wait_ge(*at("attn o", l, j - 1))
                        for k in range(nk):
                            ins = mm(bank(6, 0, P), PT_[j % 2][:, k * P:(k + 1) * P],
                                     VA[:, k * 512 + h * P:k * 512 + (h + 1) * P], k == 0, k == nk - 1)
                        done(ins, "attn pv", l, j)
                pe.wait_ge(*at("attn y", l))
                for h in range(BH):
                    for t in tiles(l):
                        ins = pe.transpose(turned(2 * h, t), OA[:, t * 512 + h * P:t * 512 + (h + 1) * P], ident)
                    done(ins, "attn y turned", l, h)
                pe.wait_ge(*at("attn y features", l, BH - 1))
                project(l, "hgrn", HF)
                pe.wait_ge(*at("hgrn copied", l, HF - 1))
                project_tokens("hgrn", xt, range(NT), "hgrn ig", l)
                pe.wait_ge(*at("hgrn ig kept", l))
                pe.wait_ge(*at("hgrn ready", l))
                for i in range(NT):
                    R = [(d, orders()[d][i], hsets[d], 4 * d) for d in range(2)]
                    for d, t, q, b0 in R:
                        if i:
                            pe.wait_ge(*at("hgrn state", l, i - 1, d))
                        pe.wait_ge(*at("hgrn scaled", l, i, d))
                        for b in range(2):
                            ins = pe.transpose(bank(b0, b * P, (b + 1) * P), q["kh"][:, b * P:(b + 1) * P], ident)
                        done(ins, "hgrn k turned", l, i, d)
                    for n in range(LEVELS + 1):
                        for d, t, q, b0 in R:
                            if n >= 2:
                                pe.wait_ge(*at("hgrn placed", l, i, d, n - 2))
                            if n == 0:
                                pe.wait_ge(*at("hgrn k kept", l, i, d))
                            if n == 1:
                                pe.wait_ge(*at("hgrn pairs", l, i, d))
                            for h in range(4):
                                rows = head_rows(h)
                                o = by_parity(b0 + 2 * (n % 2), h, 256)
                                c = (h // 2) * T + t * P
                                if n == 0:
                                    ins = mm(o, HK[d][rows, c:c + P], HQ[rows, c:c + P])
                                else:
                                    f = q["dd"][rows, (n - 1) * 256 + (h // 2) * P:(n - 1) * 256 + (h // 2 + 1) * P]
                                    ins = mm(runs(o, n - 1, 1 - d), f, runs(f, n - 1, 1 - d))
                            done(ins, "hgrn level", l, i, d, n)
                    for d, t, q, b0 in R:
                        pe.wait_ge(*at("hgrn placed", l, i, d, LEVELS))
                        for b in range(2):
                            c = slice(b * P, (b + 1) * P)
                            mm(bank(b0 + 2, b * P, (b + 1) * P), q["ktm"][:, c], HI[:, t * 256 + b * P:t * 256 + (b + 1) * P])
                        for b in range(2):
                            c = slice(b * P, (b + 1) * P)
                            mm(bank(b0 + 1, b * P, (b + 1) * P), q["qh"][:, c], q["s"][:, c], True, False)
                            for h in (2 * b, 2 * b + 1):
                                ins = mm(bank(b0 + 1, h * 64, h * 64 + 64), q["at"][:, h * P:(h + 1) * P],
                                         HI[:, t * 256 + h * 64:t * 256 + h * 64 + 64], False, True)
                        done(ins, "hgrn out", l, i, d)
                pe.wait_ge(*at("hgrn y", l))
                for b in range(2):
                    for t in tiles(l):
                        ins = pe.transpose(turned(2 * b, t), HO[:, t * 256 + b * P:t * 256 + (b + 1) * P], ident)
                done(ins, "hgrn y turned", l)
                pe.wait_ge(*at("hgrn y features", l))
                broadcast(l, "gate1", [16], streams)
                pe.wait_ge(*at("gate1 kept", l, streams[-1]))
                for half in range(2):
                    if half:
                        pe.wait_ge(*at("mixed", l, 0))
                    project_tokens("out", yt, tiles(l), "out projected", l, half)
                pe.wait_ge(*at("mixed", l, 1))
                broadcast(l, "mod2", [24, 32], streams)
                pe.wait_ge(*at("mod2 kept", l, streams[-1]))
                transpose_x(l, "ln2", tiles(l))
                pe.wait_ge(*at("ln2 modulated", l, KB - 1))
                project(l, "peer", WQ)
                pe.wait_ge(*at("peer copied", l, WQ - 1))
                for n, t in enumerate(tiles(l)):
                    if n:
                        pe.wait_ge(*at("peer scores kept", l, tiles(l)[n - 1]))
                    for j in range(2 * HEADS):
                        ins = mm(bank(j // 4, (j % 4) * P, (j % 4 + 1) * P), QT[:, j * T + t * P:j * T + (t + 1) * P],
                                 SK[:, (j % 2) * P:(j % 2 + 1) * P])
                    done(ins, "peer scores", l, t)
                pe.wait_ge(*at("peer scores kept", l, tiles(l)[-1]))
                broadcast(l, "gate2", [40], streams)

        @block.scalar
        def _(act):
            done = Steps(act, SEM["scalar_steps"], marks, True)
            params = [0]

            def load(dst, src):
                act.dma_start(dst, src).then_inc(SEM["params_loaded"], 16)
                params[0] += 16

            def copy(o, i, *name):
                done(act.activation(o, i, ACT.Copy), *name)

            def pair(b, lo=0):
                return PS[:, 512 * b + 256 + lo:512 * b + 1024]

            def stats(l, what, ts, sq):
                for t in ts:
                    if what != "ln1":
                        act.wait_ge(*at(what + " input", l, t))
                    done(act.activation(sq, x_tile(t), ACT.Copy, accum_out=ST[:, t:t + 1]), what + " sum", l, t)
                for t in ts:
                    act.wait_ge(*at(what + " mean", l, t))
                    done(act.activation(sq, x_tile(t), ACT.Square, bias=ST[:, 8 + t:9 + t],
                                        accum_out=ST[:, 16 + t:17 + t]), what + " squares", l, t)

            def rows_kept(l, what, dsts, streams):
                for s in streams:
                    act.wait_ge(*at(what + " rows", l, s))
                    for n, dst in enumerate(dsts(s)):
                        copy(dst, PS[:, 1024 * n:1024 * n + D])
                    marks[(what + " kept", l, s)] = (SEM["scalar_steps"].name, done.n)

            act.wait_ge(SEM["consts_loaded"], 48)
            done(act.activation(ST[:, 32:48], CC[:], ACT.Sigmoid), "cond sigmoid")
            act.wait_ge(SEM["x_loaded"], 32)
            for l in range(DEPTH):
                streams = [0, 1] if l + 1 < DEPTH else [0]
                ts = tiles(l)
                if l:
                    act.wait_ge(*at("final", l - 1, NT - 1))
                load(COL[:], a["cols"][l])
                load(ROW[:], a["rows"][l].partition_broadcast(P))
                load(SW[:], a["sw"][l])
                load(SK[:], a["sk"][l])
                if l == 0:
                    load(LB[:, 0:4], a["lb"])
                marks[("params", l)] = ("params_loaded", params[0])
                stats(l, "ln1", range(NT), SQ)
                for c in range(ADA // 4):
                    act.wait_ge(*at("ada rows", l, c))
                    if c >= 2:
                        act.wait_ge(*at("ada turned", l, c - 2))
                    copy(MR[c % 2], bank(5 + 2 * (c % 2))[0:2, :], "ada rows kept", l, c)
                act.wait_ge(*at("lambda sums", l))
                done(act.activation(LAM[:, 0:2], LAM[:, 0:2], ACT.Exp), "lambda exp", l)
                if l == 0:
                    act.wait_ge(*at("bounds shifted"))
                    done(act.activation(LB[:, 4:8], LB[:, 4:8], ACT.Exp), "bounds exp")
                act.wait_ge(*at("ln1 modulated", l, KB - 1))
                for c in range(RW):
                    act.wait_ge(*at("rwkv projected", l, c))
                    copy(RAW[:, c * T:(c + 1) * T], pair(2 * (c % 2)), "rwkv copied", l, c)
                done(act.activation(lo_[0:32, :], lo_[0:32, :], ACT.Tanh))
                done(act.activation(lo_[64:128, :], lo_[64:128, :], ACT.Sigmoid), "rwkv lora in", l)
                act.wait_ge(*at("rwkv conv", l))
                for b in range(2):
                    act.wait_ge(*at("rwkv kk floored", l, b))
                    done(act.activation(bv[:, b * T:(b + 1) * T], bv[:, b * T:(b + 1) * T], ACT.Sqrt), "rwkv kk root", l, b)
                for j in range(6):
                    act.wait_ge(*at("rwkv gate", l, j))
                    dst = (RA, lw0, lw1)[j // 2][:, (j % 2) * T:(j % 2 + 1) * T]
                    bias = COL[:, C_A0 + j:C_A0 + j + 1]
                    done(act.activation(dst, pair(2 * (j % 3)), ACT.Sigmoid, bias=bias), "rwkv gate read", l, j)
                act.wait_ge(*at("rwkv v turned", l))
                copy(VTM, PS[:, 0:2 * T], "rwkv v kept", l)
                for i in range(NT):
                    R = [(d, orders()[d][i], rsets[d], 4 * d) for d in range(2)]
                    for d, t, q, b0 in R:
                        act.wait_ge(*at("rwkv centred", l, i, d))
                        done(act.activation(q["em"], q["bt"], ACT.Exp, scale=0.5))
                        done(act.activation(q["tr"], q["b"], ACT.Exp))
                        done(act.activation(q["tk"], q["b"], ACT.Exp, scale=-1.0))
                        done(act.activation(q["ta"], q["ta"], ACT.Exp), "rwkv decays", l, i, d)
                    for d, t, q, b0 in R:
                        act.wait_ge(*at("rwkv abk turned", l, i, d))
                        copy(q["tm"], PS[:, 512 * b0:512 * b0 + 768], "rwkv abk kept", l, i, d)
                    for d, t, q, b0 in R:
                        act.wait_ge(*at("rwkv W", l, i, d))
                        copy(q["x2"], bank(b0 + 3, 0, 256))
                        copy(q["w"], bank(b0, 0, 256), "rwkv W kept", l, i, d)
                    for d, t, q, b0 in R:
                        act.wait_ge(*at("rwkv U", l, i, d))
                        copy(q["u"], bank(b0 + 1, 0, 256), "rwkv U kept", l, i, d)
                act.wait_ge(*at("rwkv y turned", l))
                lo = 0 if l + 1 < DEPTH else CTX
                copy(yt(0, lo), pair(0, lo))
                copy(yt(1, lo), pair(2, lo), "rwkv y features", l)
                for c in range(AQK):
                    act.wait_ge(*at("attn projected", l, c))
                    copy((QA if c < 4 else KA)[:, (c % 4) * T:(c % 4 + 1) * T], pair(2 * (c % 2)), "attn copied", l, c)
                act.wait_ge(*at("attn v", l))
                copy(VA, PS[:, 0:NT * 512], "attn v kept", l)
                jobs = [(t, h) for t in ts for h in range(BH)]
                for n in range(len(jobs) + 1):
                    if n < len(jobs):
                        keys = T if jobs[n][0] >= CT else CTX
                        c0 = 16 * (n % 2)
                        for m in range(2):
                            act.wait_ge(*at("attn max", l, n, m))
                            if m == 0 and n >= 2:
                                act.wait_ge(*at("attn a turned", l, n - 2))
                            done(act.activation(PA[n % 2][m][:, 0:keys], PS[:, 1024 * m + 256:1024 * m + 256 + keys], ACT.Exp,
                                                bias=AST[:, c0 + 2 + m:c0 + 3 + m], scale=SCALE,
                                                accum_out=AST[:, c0 + 4 + m:c0 + 5 + m]), "attn exp", l, n, m)
                    if n:
                        keys = T if jobs[n - 1][0] >= CT else CTX
                        act.wait_ge(*at("attn a turned", l, n - 1))
                        if n >= 3:
                            act.wait_ge(*at("attn pv", l, n - 3))
                        copy(PT_[(n - 1) % 2][:, 0:keys], PS[:, 2048:2048 + keys], "attn aT", l, n - 1)
                for h in range(BH):
                    act.wait_ge(*at("attn y turned", l, h))
                    copy(yt(2 + h, lo), pair(2 * h, lo), "attn y features", l, h)
                for c in range(HF):
                    act.wait_ge(*at("hgrn projected", l, c))
                    copy(AR[:, c * T:(c + 1) * T], pair(2 * (c % 2)), "hgrn copied", l, c)
                act.wait_ge(*at("hgrn ig", l))
                ig = PS[:, 0:NT * 512].rearrange("p (t two c) -> p t two c", t=NT, two=2)
                copy(split(HI, NT), ig[:, :, 0, :])
                copy(split(HG, NT), ig[:, :, 1, :], "hgrn ig kept", l)
                done(act.activation(HS, HQ, ACT.Sigmoid), "hgrn q gate", l)
                for d in range(2):
                    done(act.activation(HK[d], HZ[d], ACT.Sigmoid, scale=-1.0))
                    done(act.activation(HZ[d], HZ[d], ACT.Sigmoid), "hgrn gates", l, d)
                for d in range(2):
                    act.wait_ge(*at("hgrn f", l, d))
                    done(act.activation(HZ[d], HZ[d], ACT.Ln), "hgrn log", l, d)
                for i in range(NT):
                    R = [(d, orders()[d][i], hsets[d], 4 * d) for d in range(2)]
                    for d, t, q, b0 in R:
                        act.wait_ge(*at("hgrn sums", l, i, d))
                        done(act.activation(q["eb"], q["b"], ACT.Exp))
                        done(act.activation(q["kh"], q["kh"], ACT.Exp))
                        done(act.activation(q["el"], q["bl"], ACT.Exp), "hgrn decays", l, i, d)
                        act.wait_ge(*at("hgrn differences", l, i, d))
                        done(act.activation(q["dd"], q["dd"], ACT.Abs))
                        done(act.activation(q["dd"], q["dd"], ACT.Exp, scale=-1.0), "hgrn level decays", l, i, d)
                    for d, t, q, b0 in R:
                        act.wait_ge(*at("hgrn k turned", l, i, d))
                        copy(q["ktm"], bank(b0, 0, 256), "hgrn k kept", l, i, d)
                done(act.activation(HS, HG, ACT.Sigmoid), "hgrn g gate", l)
                act.wait_ge(*at("hgrn y turned", l))
                copy(yt(6, lo), pair(0, lo))
                copy(yt(7, lo), pair(2, lo), "hgrn y features", l)
                act.dma_start(LNR[0], a["ln"][l, 0].partition_broadcast(P)).then_inc(SEM["ln_rows_loaded"], 16)
                act.dma_start(LNR[1], a["ln"][l, 1].partition_broadcast(P)).then_inc(SEM["ln_rows_loaded"], 16)
                rows_kept(l, "gate1", lambda s: [BC[s]], streams)
                stats(l, "mix", ts, SQ)
                act.wait_ge(*at("mixed", l, 1))
                rows_kept(l, "mod2", lambda s: [BC[2 * s], BC[2 * s + 1]], streams)
                stats(l, "ln2", ts, SQ)
                act.wait_ge(*at("peer input", l))
                for c in range(WQ):
                    act.wait_ge(*at("peer projected", l, c))
                    copy(QT[:, c * T + lo:(c + 1) * T], pair(2 * (c % 2), lo), "peer copied", l, c)
                for t in ts:
                    act.wait_ge(*at("peer scores", l, t))
                    if t != ts[0]:
                        act.wait_ge(*at("routed", l, t - 1))
                    copy(SC, PS[:, 0:2048], "peer scores kept", l, t)
                    act.wait_ge(*at("peer centred", l, t))
                    done(act.activation(TOP, TOP, ACT.Exp), "peer exp", l, t)
                act.wait_ge(*at("routed", l, ts[-1]))
                rows_kept(l, "gate2", lambda s: [G2[s]], streams)
                act.dma_start(LNR2[0], a["ln"][l, 2].partition_broadcast(P)).then_inc(SEM["ln_rows_loaded"], 16)
                act.dma_start(LNR2[1], a["ln"][l, 3].partition_broadcast(P)).then_inc(SEM["ln_rows_loaded"], 16)
                for n, t in enumerate(ts):
                    base = (l * NT + n) * ITER
                    with act.Fori(0, ITER) as i:
                        for g in range(2):
                            c = slice(GROUP * g, GROUP * g + GROUP)
                            act.wait_ge(SEM["expert_steps"], (i + base) * (2 * GSTEP) + (GSTEP + g * GSTEP + GROUP))
                            act.activation(GEL[:, c], DOT[:, c], ACT.Gelu).then_inc(SEM["gelu_done"], 1)
                stats(l, "fin", ts, SQ2)

        @block.gpsimd
        def _(pool):
            done = Steps(pool, SEM["pool_steps"], marks, True)

            def rsqrt(ap, *name):
                pool.wait_ge(*at("plus eps", *name))
                done(pool.tensor_tensor(ap, ap, cf(K_HALF, 1).broadcast_to([P, ap.shape[-1]]), ALU.pow), "rsqrt", *name)

            for l in range(DEPTH):
                ts = tiles(l)
                for t in range(NT):
                    rsqrt(ST[:, 16 + t:17 + t], "ln1", l, t)
                for i in range(NT):
                    for d in range(2):
                        q = rsets[d]
                        if i == 0:
                            pool.wait_ge(*at("rwkv conv", l))
                        else:
                            pool.wait_ge(*at("rwkv out", l, i - 1, d))
                        done(pool.tensor_copy(split(q["T"], 4), rep(ident, 4)))
                        done(pool.tensor_copy(split(q["G"], 4), rep(ident, 4)), "rwkv TG", l, i, d)
                rsqrt(RM[:, 24:48], "group norm", l)
                rsqrt(AST[:, 32:32 + 4 * len(ts)], "attn norm", l)
                rsqrt(HM, "hgrn norm", l)
                for what in ("mix", "ln2"):
                    for t in ts:
                        rsqrt(ST[:, 16 + t:17 + t], what, l, t)
                for n, t in enumerate(ts):
                    if n == 0:
                        pool.wait_ge(*at("routed", l, ts[-1]))
                        pool.wait_ge(*at("gate2 kept", l, 0))
                    base = (l * NT + n) * ITER
                    with pool.Fori(0, ITER) as i:
                        for g in range(2):
                            c = slice(GROUP * g, GROUP * g + GROUP)
                            pool.wait_ge(SEM["expert_steps"], (i + base) * (2 * GSTEP) + g * GSTEP)
                            pool.tensor_copy(IDS[:, c], IDX[:, bass.ds(i * (2 * GROUP) + (t * P + g * GROUP), GROUP)])\
                                .then_inc(SEM["ids_staged"], 1)
                            pool.wait_ge(SEM["ids_staged"], (i + base) * 2 + (g + 1))
                            pool.tensor_tensor(DUM, ident[:, 0:1], ident[:, 0:1], ALU.mult)
                            for k in range(GROUP):
                                s = g * GROUP + k
                                pool.indirect_dma_start(GB[s], None, a["uv"], IndirectOffsetOnAxis(ap=IDS[:, s:s + 1], axis=0))\
                                    .then_inc(rows_in[s], 16)
                for t in ts:
                    rsqrt(ST[:, 16 + t:17 + t], "fin", l, t)

        @block.vector
        def _(dve):
            done = Steps(dve, SEM["vector_steps"], marks, True)

            def tt(o, x, y, op, *name):
                done(dve.tensor_tensor(o, x, y, op), *name)

            def ts1(o, x, s, op, *name):
                done(dve.tensor_scalar(o, x, s, None, op), *name)

            def ts2(o, x, s, r, op0, op1, *name):
                done(dve.tensor_scalar(o, x, s, r, op0, op1), *name)

            def stt(o, x, s, y, op0, op1, *name):
                done(dve.scalar_tensor_tensor(out=o, in0=x, scalar=s, in1=y, op0=op0, op1=op1), *name)

            def copy(o, x, *name):
                done(dve.tensor_copy(o, x), *name)

            def zero(o, *name):
                done(dve.memset(o, 0.0), *name)

            def rsqrt(ap, scale, eps, *name):
                ts2(ap, ap, scale, eps, ALU.mult, ALU.add, "plus eps", *name)
                dve.wait_ge(*at("rsqrt", *name))

            def normed(l, what, ts, dst):
                for t in ts:
                    dve.wait_ge(*at(what + " sum", l, t))
                    ts1(ST[:, 8 + t:9 + t], ST[:, t:t + 1], -1.0 / D, ALU.mult, what + " mean", l, t)
                for t in ts:
                    dve.wait_ge(*at(what + " squares", l, t))
                    rsqrt(ST[:, 16 + t:17 + t], 1.0 / D, EPS, what, l, t)
                    ts2(dst(t), x_tile(t), ST[:, 8 + t:9 + t], ST[:, 16 + t:17 + t], ALU.add, ALU.mult, what + " normed", l, t)

            def modulated(l, what, ts, sc, sh):
                for k in range(KB):
                    dve.wait_ge(*at(what + " turned", l, k))
                    p = 1024 * (k % 3) + 256
                    for s, lo, hi in ((1, 0, CTX), (0, CTX, T)):
                        if s == 1 and ts[0]:
                            continue
                        c, h = 2 * (sc + k) + s, 2 * (sh + k) + s
                        ts2(xt(k, lo, hi), PS[:, p + lo:p + hi], MC[:, c:c + 1], MC[:, h:h + 1], ALU.mult, ALU.add,
                            what + " modulated", l, k)

            def head_norm(o, m, n, w, scratch, eps, *name):
                tt(scratch, o, o, ALU.mult)
                done(dve.tensor_reduce(m, split(scratch, n), AX.X, ALU.add))
                rsqrt(m, 1.0 / w, eps, *name)
                tt(split(o, n), split(o, n), spread(m, w), ALU.mult)

            dve.wait_ge(*at("cond sigmoid"))
            tt(CC[:], CC[:], ST[:, 32:48], ALU.mult, "cond silu")
            for l in range(DEPTH):
                ts = tiles(l)
                normed(l, "ln1", range(NT), lambda t: XN[:, t * D:(t + 1) * D])
                dve.wait_ge(*at("params", l))
                LV = ROW[:, R_LAM:R_LAM + 256]
                for n in range(2):
                    done(dve.tensor_tensor_reduce(out=LV[:, n * 128:n * 128 + 64], in0=LV[:, n * 128:n * 128 + 64],
                                                  in1=LV[:, n * 128 + 64:n * 128 + 128], scale=1.0, scalar=0.0,
                                                  op0=ALU.mult, op1=ALU.add, accum_out=LAM[:, n:n + 1]), "lambda sums", l)
                dve.wait_ge(*at("lambda exp", l))
                tt(LAM[:, 2:3], LAM[:, 1:2], LAM[:, 0:1], ALU.subtract)
                lam_init = 0.8 - 0.6 * math.exp(-0.3 * l)
                ts1(LAM[:, 2:3], LAM[:, 2:3], -lam_init, ALU.add)
                if l == 0:
                    tt(LB[:, 8:10], LB[:, 0:2], LB[:, 2:4], ALU.max)
                    tt(LB[:, 4:6], LB[:, 0:2], LB[:, 8:10], ALU.subtract)
                    tt(LB[:, 6:8], LB[:, 2:4], LB[:, 8:10], ALU.subtract, "bounds shifted")
                    dve.wait_ge(*at("bounds exp"))
                    tt(LB[:, 8:10], LB[:, 4:6], LB[:, 6:8], ALU.add)
                    done(dve.reciprocal(LB[:, 8:10], LB[:, 8:10]))
                    tt(LB[:, 4:6], LB[:, 4:6], LB[:, 8:10], ALU.mult)
                    tt(LB[:, 6:8], LB[:, 6:8], LB[:, 8:10], ALU.mult)
                    tt(LB[:, 6:8], LB[:, 6:8], LB[:, 4:6], ALU.add)
                    tt(LB[:, 8:10], LB[:, 4:6], LB[:, 4:6], ALU.subtract)
                    tt(LB[:, 10:12], LB[:, 6:8], LB[:, 4:6], ALU.subtract)
                    ts2(LB[:, 12:16], LB[:, 8:12], -1.0, 1.0, ALU.mult, ALU.add)
                dve.wait_ge(*at("ada turned", l, ADA // 4 - 1))
                tt(MC[:].rearrange("p (n s) -> p n s", s=2), bank(6, 0, 96).rearrange("p (n s) -> p n s", s=2),
                   spread(COL[:, C_ADAB:C_ADAB + ADA], 2), ALU.add)
                for c in (8, 32):
                    ts1(MC[:, 2 * c:2 * c + 16], MC[:, 2 * c:2 * c + 16], 1.0, ALU.add, "mod cols", l)
                modulated(l, "ln1", range(NT), 8, 0)
                for c in range(6):
                    dve.wait_ge(*at("rwkv copied", l, c))
                    x, y = RAW[:, c * T:(c + 1) * T], CV[:, c * T:(c + 1) * T]
                    w = [COL[:, C_CONV + 6 * j + c:C_CONV + 6 * j + c + 1] for j in range(3)]
                    ts1(y, x, w[1], ALU.mult)
                    for lo, hi in ((0, CTX), (CTX, T)):
                        stt(y[:, lo + 1:hi], x[:, lo:hi - 1], w[0], y[:, lo + 1:hi], ALU.mult, ALU.add)
                        stt(y[:, lo:hi - 1], x[:, lo + 1:hi], w[2], y[:, lo:hi - 1], ALU.mult, ALU.add, "rwkv conv", l)
                blk = lambda ap, b: ap[:, b * T:(b + 1) * T]
                for b in range(2):
                    ts1(blk(nkk, b), blk(k_, b), COL[:, C_KK + b:C_KK + b + 1], ALU.mult)
                tt(bv, nkk, nkk, ALU.mult, "rwkv kk squared", l)
                for b in range(2):
                    dve.wait_ge(*at("rwkv kk norm", l, b))
                    ts1(blk(bv, b), PS[:, 1024 * b + 256:1024 * b + 1024], 1e-24, ALU.max, "rwkv kk floored", l, b)
                for b in range(2):
                    dve.wait_ge(*at("rwkv kk root", l, b))
                    done(dve.reciprocal(blk(bv, b), blk(bv, b)))
                stt(nkk, nkk, -1.0, bv, ALU.mult, ALU.mult, "rwkv kk", l)
                dve.wait_ge(*at("rwkv gate read", l, 5))
                ts2(RM[:, 0:2], COL[:, C_KA:C_KA + 2], -1.0, 1.0, ALU.mult, ALU.add)
                for b in range(2):
                    ts2(blk(bv, b), blk(RA, b), COL[:, C_KA + b:C_KA + b + 1], RM[:, b:b + 1], ALU.mult, ALU.add)
                tt(k_, k_, bv, ALU.mult)
                stt(bv, nkk, -1.0, RA, ALU.mult, ALU.mult)
                for b in range(2):
                    stt(blk(RA, b), blk(r_, b), COL[:, C_RK + b:C_RK + b + 1], blk(k_, b), ALU.mult, ALU.mult, "rwkv rk", l)
                for d in range(2):
                    ts1(lw_[d], lw_[d], -math.exp(-0.5), ALU.mult)
                dve.wait_ge(*at("rwkv bonus", l))
                copy(BON, bank(7, 0, 24))
                for d in range(2):
                    zero(rsets[d]["s"])
                    for n in ("abT", "akT", "qbT", "qkT"):
                        zero(rsets[d][n])
                dve.wait_ge(*at("rwkv v turned", l))
                zero(RO, "rwkv ready", l)
                for i in range(NT):
                    R = [(d, orders()[d][i], rsets[d], 4 * d) for d in range(2)]
                    for d, t, q, b0 in R:
                        lw = split(lw_[d], 2)[:, :, t * P:(t + 1) * P]
                        for b in range(2):
                            o, x = q["b"][:, b * P:(b + 1) * P], lw_[d][:, b * T + t * P:b * T + (t + 1) * P]
                            if d:
                                o, x = o[:, ::-1], x[:, ::-1]
                            done(dve.tensor_tensor_scan(o, cf(K_ONES), x, 0.0, ALU.mult, ALU.add))
                        end = 0 if d else P - 1
                        copy(q["bt"].unsqueeze(2), split(q["b"], 2)[:, :, end:end + 1])
                        ts1(q["mc"], q["bt"], -0.5, ALU.mult)
                        tt(split(q["b"], 2), split(q["b"], 2), spread(q["mc"], P), ALU.add)
                        tt(split(q["ta"], 2), split(q["b"], 2), lw, ALU.subtract, "rwkv centred", l, i, d)
                    for d, t, q, b0 in R:
                        sl = lambda ap: split(ap, 2)[:, :, t * P:(t + 1) * P]
                        dve.wait_ge(*at("rwkv decays", l, i, d))
                        tt(split(q["ta"], 2), split(q["ta"], 2), sl(nkk), ALU.mult)
                        tt(split(q["tr"], 2), split(q["tr"], 2), sl(r_), ALU.mult)
                        tt(split(q["tb"], 2), split(q["tk"], 2), sl(bv), ALU.mult)
                        tt(split(q["tk"], 2), split(q["tk"], 2), sl(k_), ALU.mult)
                        tt(split(q["sm"], 2), split(q["s"], 2), spread(q["em"], P), ALU.mult, "rwkv scaled", l, i, d)
                    for d, t, q, b0 in R:
                        for n, (buf, m) in enumerate((("abT", B_STRICT), ("akT", B_STRICT), ("qbT", B_INCL), ("qkT", B_INCL))):
                            dve.wait_ge(*at("rwkv scores", l, i, d, n // 2 * 2 + 1))
                            done(dve.copy_predicated(parity_heads(q[buf]), rep4(mask(m + d)), parity_banks(b0 + n // 2 * 2, n % 2 * 256)),
                                 "rwkv scores kept", l, i, d)
                    for lev in range(LEVELS):
                        for d, t, q, b0 in R:
                            dve.wait_ge(*at("rwkv AT", l, i, d, lev))
                            inv = cf(K_INV + (d * LEVELS + lev) * P)
                            if lev == 0:
                                tt(parity_heads(q["X"]), parity_banks(b0, 0), rep4(inv), ALU.mult, "rwkv X", l, i, d, lev)
                            else:
                                tt(split(q["X"], 4), split(bank(b0), 4), rep(inv, 4), ALU.mult, "rwkv X", l, i, d, lev)
                        for d, t, q, b0 in R:
                            dve.wait_ge(*at("rwkv dT", l, i, d, lev))
                            if lev == 0:
                                dve.wait_ge(*at("rwkv TG", l, i, d))
                            left, right = (0, 1) if d == 0 else (1, 0)
                            if lev < LEVELS - 1:
                                v = runs(q["T"], lev, left)
                                tt(v, v, runs(bank(b0 + 1), lev, left), ALU.add, "rwkv T", l, i, d, lev)
                            v = runs(q["G"], lev, right)
                            tt(v, v, runs(bank(b0 + 2), lev, right), ALU.add, "rwkv G", l, i, d, lev)
                    for d, t, q, b0 in R:
                        dve.wait_ge(*at("rwkv out", l, i, d))
                        tt(split(q["x2"], 2), split(bank(b0 + 3, 256, 512), 2), rep(cf(K_BD), 2), ALU.mult)
                        tt(q["x2"], q["x2"], q["sm"], ALU.add)
                        tt(split(q["s"], 2), split(q["x2"], 2), spread(q["em"], P), ALU.mult)
                        o = RO[:, t * 256:(t + 1) * 256]
                        tt(o, o, bank(b0 + 2, 0, 256), ALU.add, "rwkv state", l, i, d)
                done(dve.tensor_reduce(RM[:, 0:24], split(RO, 24), AX.X, ALU.add))
                ts1(RM[:, 0:24], RM[:, 0:24], 1.0 / HD, ALU.mult)
                tt(split(RO, 24), split(RO, 24), spread(RM[:, 0:24], HD), ALU.subtract)
                head_norm(RO, RM[:, 24:48], 24, HD, RA, GN_EPS, "group norm", l)
                tt(split(RO, NT), split(RO, NT), rep(ROW[:, R_GNW:R_GNW + 256], NT), ALU.mult)
                tt(split(RO, NT), split(RO, NT), rep(ROW[:, R_GNB:R_GNB + 256], NT), ALU.add)
                tt(split(RA, 24), split(VTM, 24), spread(BON, HD), ALU.mult)
                tt(RO, RO, RA, ALU.add)
                dve.wait_ge(*at("rwkv g", l))
                tt(RO, RO, PS[:, 0:NT * 256], ALU.mult, "rwkv y", l)
                for n in range(8):
                    dve.wait_ge(*at("rotated", l, n))
                    if n == 0:
                        dve.wait_ge(*at("attn copied", l, AQK - 1))
                    x = (QA if n < 4 else KA)[:, (n % 4) * T + CTX:(n % 4 + 1) * T]
                    tt(RT, bank(6 + n % 2), cf(K_SIN, SEQ), ALU.mult)
                    tt(x, x, cf(K_COS, SEQ), ALU.mult)
                    tt(x, x, RT, ALU.add, "rope", l, n)
                jobs = [(t, h) for t in ts for h in range(BH)]
                for n in range(len(jobs) + 2):
                    if 1 <= n <= len(jobs):
                        j = n - 1
                        keys = T if jobs[j][0] >= CT else CTX
                        c0 = 16 * (j % 2)
                        p0, p1 = (PA[j % 2][m][:, 0:keys] for m in range(2))
                        dve.wait_ge(*at("attn exp", l, j, 1))
                        done(dve.reciprocal(AST[:, c0 + 6:c0 + 8], AST[:, c0 + 4:c0 + 6]))
                        tt(AST[:, c0 + 8:c0 + 9], AST[:, c0 + 7:c0 + 8], LAM[:, 2:3], ALU.mult)
                        ts1(p0, p0, AST[:, c0 + 6:c0 + 7], ALU.mult)
                        stt(p0, p1, AST[:, c0 + 8:c0 + 9], p0, ALU.mult, ALU.add, "attn a", l, j)
                    if n < len(jobs):
                        keys = T if jobs[n][0] >= CT else CTX
                        c0 = 16 * (n % 2)
                        for m in range(2):
                            dve.wait_ge(*at("attn scores", l, n, m))
                            done(dve.tensor_reduce(AST[:, c0 + m:c0 + m + 1], PS[:, 1024 * m + 256:1024 * m + 256 + keys],
                                                   AX.X, ALU.max))
                            ts1(AST[:, c0 + 2 + m:c0 + 3 + m], AST[:, c0 + m:c0 + m + 1], -SCALE, ALU.mult, "attn max", l, n, m)
                    if n >= 2:
                        j = n - 2
                        t, h = jobs[j]
                        dve.wait_ge(*at("attn pv", l, j))
                        copy(OA[:, t * 512 + h * P:t * 512 + (h + 1) * P], bank(6, 0, P), "attn o", l, j)
                n0, nt = ts[0], len(ts)
                head_norm(OA[:, n0 * 512:], AST[:, 32:32 + 4 * nt], 4 * nt, P, OS[:, 0:nt * 512], EPS, "attn norm", l)
                o = split(OA[:, n0 * 512:], 4 * nt)
                tt(o, o, rep(ROW[:, R_SUB:R_SUB + P], 4 * nt), ALU.mult)
                ts1(OA[:, n0 * 512:], OA[:, n0 * 512:], 1.0 - lam_init, ALU.mult, "attn y", l)
                dve.wait_ge(*at("hgrn q gate", l))
                tt(HQ, HQ, HS, ALU.mult)
                big = float(2.0 ** LN_SHIFT)
                for d in range(2):
                    dve.wait_ge(*at("hgrn gates", l, d))
                    for b in range(2):
                        lb, om = LB[:, 8 + 2 * l + b:9 + 2 * l + b], LB[:, 12 + 2 * l + b:13 + 2 * l + b]
                        ts2(blk(HZ[d], b), blk(HZ[d], b), om, lb, ALU.mult, ALU.add)
                        ts1(blk(HK[d], b), blk(HK[d], b), om, ALU.mult)
                    ts1(HZ[d], HZ[d], MIN_FORGET, ALU.max)
                    ts2((HO, HS)[d], HZ[d], 1.0 / big, big - 1.0, ALU.is_lt, ALU.mult)
                    stt(HZ[d], (HO, HS)[d], 1.0, HZ[d], ALU.add, ALU.mult, "hgrn f", l, d)
                for d in range(2):
                    dve.wait_ge(*at("hgrn log", l, d))
                    stt(HZ[d], (HO, HS)[d], -LN_SHIFT * math.log(2.0) / big, HZ[d], ALU.mult, ALU.add)
                    zero(hsets[d]["s"])
                    zero(hsets[d]["at"])
                zero(HO, "hgrn ready", l)
                for i in range(NT):
                    R = [(d, orders()[d][i], hsets[d], 4 * d) for d in range(2)]
                    for d, t, q, b0 in R:
                        if i:
                            dve.wait_ge(*at("hgrn out", l, i - 1, d))
                        for b in range(2):
                            o, x = q["b"][:, b * P:(b + 1) * P], HZ[d][:, b * T + t * P:b * T + (t + 1) * P]
                            if d:
                                o, x = o[:, ::-1], x[:, ::-1]
                            done(dve.tensor_tensor_scan(o, cf(K_ONES), x, 0.0, ALU.mult, ALU.add))
                        end = 0 if d else P - 1
                        copy(q["bl"].unsqueeze(2), split(q["b"], 2)[:, :, end:end + 1])
                        tt(split(q["kh"], 2), spread(q["bl"], P), split(q["b"], 2), ALU.subtract, "hgrn sums", l, i, d)
                        for lev in range(LEVELS):
                            m = 1 << lev
                            v = q["b"].rearrange("p (n m) -> p n m", m=2 * m)
                            ref = v[:, :, m - 1 + d:m + d].broadcast_to([P, P // m, 2 * m])
                            o = q["dd"][:, lev * 256:(lev + 1) * 256].rearrange("p (n m) -> p n m", m=2 * m)
                            tt(o, v, ref, ALU.subtract, "hgrn differences", l, i, d)
                    for d, t, q, b0 in R:
                        sl = lambda ap: split(ap, 2)[:, :, t * P:(t + 1) * P]
                        dve.wait_ge(*at("hgrn decays", l, i, d))
                        tt(split(q["qh"], 2), split(q["eb"], 2), sl(HQ), ALU.mult)
                        tt(split(q["kh"], 2), split(q["kh"], 2), sl(HK[d]), ALU.mult, "hgrn scaled", l, i, d)
                        dve.wait_ge(*at("hgrn level decays", l, i, d))
                        for lev in range(LEVELS):
                            for b in range(2):
                                f = q["dd"][:, lev * 256 + b * P:lev * 256 + (b + 1) * P]
                                c = b * T + t * P
                                for src, half in ((HQ, 1 - d), (HK[d], d)):
                                    tt(runs(f, lev, half), runs(f, lev, half), runs(src[:, c:c + P], lev, half), ALU.mult,
                                       "hgrn pairs", l, i, d)
                    for n in range(LEVELS + 1):
                        for d, t, q, b0 in R:
                            dve.wait_ge(*at("hgrn level", l, i, d, n))
                            src = parity_banks(b0 + 2 * (n % 2), 256)
                            if n == 0:
                                done(dve.copy_predicated(parity_heads(q["at"]), rep4(mask(B_DIAG)), src),
                                     "hgrn placed", l, i, d, n)
                            else:
                                lev = n - 1
                                mk = runs(mask(B_LEV + d * LEVELS + lev), lev, 1 - d)
                                for par in range(2):
                                    for b in range(2):
                                        c = (2 * b + par) * P
                                        done(dve.copy_predicated(runs(q["at"][:, c:c + P], lev, 1 - d), mk,
                                                                 runs(src[:, par, b, :], lev, 1 - d)),
                                             "hgrn placed", l, i, d, n)
                    for d, t, q, b0 in R:
                        dve.wait_ge(*at("hgrn out", l, i, d))
                        tt(split(q["s1"], 2), split(bank(b0 + 2, 0, 256), 2), rep(cf(K_BD), 2), ALU.mult)
                        tt(split(q["s"], 2), split(q["s"], 2), spread(q["el"], P), ALU.mult)
                        tt(q["s"], q["s"], q["s1"], ALU.add)
                        o = HO[:, t * 256:(t + 1) * 256]
                        tt(o, o, bank(b0 + 1, 0, 256), ALU.add, "hgrn state", l, i, d)
                head_norm(HO, HM, 24, HD, HK[0], EPS, "hgrn norm", l)
                tt(split(HO, 24), split(HO, 24), rep(ROW[:, R_HN:R_HN + HD], 24), ALU.mult)
                dve.wait_ge(*at("hgrn g gate", l))
                tt(HG, HG, HS, ALU.mult)
                tt(HO, HO, HG, ALU.mult, "hgrn y", l)
                dve.wait_ge(*at("gate1 kept", l, 1 if l + 1 < DEPTH else 0))
                for half in range(2):
                    dve.wait_ge(*at("out projected", l, half))
                    for n, t in enumerate(ts):
                        c = slice(half * 512, half * 512 + 512)
                        y = XN[:, t * D:(t + 1) * D][:, c]
                        tt(y, bank(n), BC[1 if t < CT else 0][:, c], ALU.mult)
                        stt(x_tile(t)[:, c], x_tile(t)[:, c], ALPHA, y, ALU.mult, ALU.add, "mixed", l, half)
                        marks[("mix input", l, t)] = marks[("mixed", l, half)]
                normed(l, "mix", ts, lambda t: XN[:, t * D:(t + 1) * D])
                dve.wait_ge(SEM["ln_rows_loaded"], 64 * l + 32)
                for t in ts:
                    xn = XN[:, t * D:(t + 1) * D]
                    tt(xn, xn, LNR[0], ALU.mult)
                    tt(x_tile(t), xn, LNR[1], ALU.add, "ln2 input", l, t)
                normed(l, "ln2", ts, lambda t: XN[:, t * D:(t + 1) * D])
                dve.wait_ge(*at("mod2 kept", l, 1 if l + 1 < DEPTH else 0))
                dve.wait_ge(*at("out projected", l, 1))
                for t in ts:
                    s = 1 if t < CT else 0
                    u = U2[:, t * D:(t + 1) * D]
                    tt(u, XN[:, t * D:(t + 1) * D], BC[2 * s + 1], ALU.mult)
                    tt(u, u, BC[2 * s], ALU.add)
                modulated(l, "ln2", ts, 32, 24)
                marks[("peer input", l)] = marks[("ln2 modulated", l, KB - 1)]
                for t in ts:
                    dve.wait_ge(*at("peer scores kept", l, t))
                    for j in range(2 * HEADS):
                        s = SC[:, j * P:(j + 1) * P]
                        top16(dve, done, s, SV[:, j * 16:j * 16 + 16], SI[:, j * 16:j * 16 + 16])
                    copy(SIF, SI)
                    sv = SV.rearrange("p (h two k) -> p h two k", h=HEADS, two=2)
                    for h in range(HEADS):
                        c = CAND[:, h * 256:(h + 1) * 256].rearrange("p (i j) -> p i j", i=16)
                        tt(c, spread(sv[:, h, 0, :], 16), rep(sv[:, h, 1, :], 16), ALU.add)
                    for h in range(HEADS):
                        top16(dve, done, CAND[:, h * 256:(h + 1) * 256], TOP[:, h * 16:h * 16 + 16], CI[:, h * 16:h * 16 + 16])
                    done(dve.tensor_single_scalar(CIJ[:, 0:P], CI, 4, ALU.logical_shift_right))
                    done(dve.tensor_single_scalar(CIJ[:, P:2 * P], CI, 15, ALU.bitwise_and))
                    copy(CF2, CIJ)
                    sif = SIF.rearrange("p (h two k) -> p h two k", h=HEADS, two=2)
                    for half in range(2):
                        tt(split(OH, P), spread(CF2[:, half * P:(half + 1) * P], 16), rep(cf(K_IOTA, 16), P), ALU.is_equal)
                        for h in range(HEADS):
                            o = OH[:, h * 256:(h + 1) * 256].rearrange("p (k i) -> p k i", i=16)
                            tt(o, o, rep(sif[:, h, half, :], 16), ALU.mult)
                        done(dve.tensor_reduce(E0[:, half * P:(half + 1) * P], split(OH, P), AX.X, ALU.add))
                    stt(E0[:, 0:P], E0[:, 0:P], float(NKEYS), E0[:, P:2 * P], ALU.mult, ALU.add)
                    ts1(E0[:, 0:P], E0[:, 0:P], float(l * EXPERTS), ALU.add)
                    copy(IDX[:, t * P:(t + 1) * P], E0[:, 0:P])
                    for h in range(HEADS):
                        ts1(E0[:, P + h:P + h + 1], TOP[:, h * 16:h * 16 + 1], 1.0, ALU.mult)
                    tt(split(TOP, HEADS), split(TOP, HEADS), spread(E0[:, P:P + HEADS], 16), ALU.subtract, "peer centred", l, t)
                    dve.wait_ge(*at("peer exp", l, t))
                    done(dve.tensor_reduce(GS[:, 0:HEADS], split(TOP, HEADS), AX.X, ALU.add))
                    done(dve.reciprocal(GS[:, 0:HEADS], GS[:, 0:HEADS]))
                    tt(split(GATE[:, t * P:(t + 1) * P], HEADS), split(TOP, HEADS), spread(GS[:, 0:HEADS], 16), ALU.mult,
                       "routed", l, t)
                step = SEM["expert_steps"]
                if l == 0:
                    dve.sem_inc(step, GSTEP)
                for n, t in enumerate(ts):
                    base = (l * NT + n) * ITER
                    zero(ACC)
                    u = U2[:, t * D:(t + 1) * D]
                    with dve.Fori(0, ITER) as i:
                        for g in range(2):
                            c0 = g * GROUP
                            first = (i + base) * (2 * GSTEP) + (1 + g) * GSTEP
                            for k in range(GROUP):
                                s = c0 + k
                                dve.wait_ge(rows_in[s], (i + base) * 16 + 16)
                                dve.wait_ge(step, first + k)
                                dve.tensor_tensor_reduce(out=JUNK, in0=GB[s][:, 0:D], in1=u, scale=1.0, scalar=0.0,
                                                         op0=ALU.mult, op1=ALU.add, accum_out=DOT[:, s:s + 1]).then_inc(step, 1)
                            dve.wait_ge(SEM["gelu_done"], (i + base) * 2 + (g + 1))
                            dve.tensor_tensor(WGT[:, c0:c0 + GROUP], GEL[:, c0:c0 + GROUP],
                                              GATE[:, bass.ds(i * (2 * GROUP) + (t * P + c0), GROUP)], ALU.mult).then_inc(step, 1)
                            for k in range(GROUP):
                                s = c0 + k
                                dve.wait_ge(step, first + (GROUP + 1 + k))
                                dve.scalar_tensor_tensor(out=ACC, in0=GB[s][:, D:2 * D], scalar=WGT[:, s:s + 1], in1=ACC,
                                                         op0=ALU.mult, op1=ALU.add).then_inc(step, 1)
                    dve.wait_ge(step, (base + ITER) * 2 * GSTEP + GSTEP)
                    dve.wait_ge(*at("gate2 kept", l, 0 if l + 1 == DEPTH else 1))
                    tt(ACC, ACC, G2[1 if t < CT else 0], ALU.mult)
                    stt(x_tile(t), x_tile(t), ALPHA, ACC, ALU.mult, ALU.add, "peer mixed", l, t)
                    marks[("fin input", l, t)] = marks[("peer mixed", l, t)]
                normed(l, "fin", ts, x_tile)
                dve.wait_ge(SEM["ln_rows_loaded"], 64 * l + 64)
                for t in ts:
                    tt(x_tile(t), x_tile(t), LNR2[0], ALU.mult)
                    tt(x_tile(t), x_tile(t), LNR2[1], ALU.add, "final", l, t)


def top16(dve, done, s, values, places):
    done(dve.max(values[:, 0:8], s))
    done(dve.max_index(places[:, 0:8], values[:, 0:8], s))
    done(dve.match_replace(s, values[:, 0:8], s, -3.0e38))
    done(dve.max(values[:, 8:16], s))
    done(dve.max_index(places[:, 8:16], values[:, 8:16], s))


def constants():
    f = np.zeros((P, NCF), np.float32)
    p = np.arange(P)
    f[:, K_ID:K_ID + P] = np.eye(P)
    for d in range(P):
        s = d + 16 if d % 32 < 16 else d - 16
        f[s, K_ROT + d] = -1.0 if d % 32 < 16 else 1.0
    f[:, K_ONES:K_ONES + P] = 1.0
    f[:, K_BD:K_BD + P] = (p[:, None] // 64 == p[None, :] // 64)
    n = np.arange(SEQ)
    inv = (10000.0 ** (-2.0 * np.arange(16, dtype=np.float32) / 32.0)).astype(np.float32)
    row, col = (n // GRID_W).astype(np.float32), (n % GRID_W).astype(np.float32)
    ang = np.where((p[:, None] % 64 < 32), row[None, :], col[None, :]).astype(np.float32) * inv[p % 16][:, None]
    f[:, K_COS:K_COS + SEQ] = np.cos(ang)
    f[:, K_SIN:K_SIN + SEQ] = np.sin(ang)
    f[:, K_IOTA:K_IOTA + 16] = np.arange(16)
    f[:, K_HSEL:K_HSEL + 2] = (p[:, None] // 64 == np.arange(2)[None, :])
    f[:, K_HALF] = -0.5
    b = np.zeros((P, NCB, P), np.uint8)
    s, t = p[:, None], p[None, :]
    for lev in range(LEVELS):
        same = ((s ^ t) >> lev) == 1
        b[:, B_LEV + lev] = same & (s < t)
        b[:, B_LEV + LEVELS + lev] = same & (s > t)
        f[:, K_INV + lev * P:K_INV + (lev + 1) * P] = same & (s > t)
        f[:, K_INV + (LEVELS + lev) * P:K_INV + (LEVELS + lev + 1) * P] = same & (s < t)
    b[:, B_DIAG] = s == t
    b[:, B_STRICT], b[:, B_STRICT + 1] = s < t, s > t
    b[:, B_INCL], b[:, B_INCL + 1] = s <= t, s >= t
    return f, b.reshape(P, NCB * P).view(np.uint32)


def feature_pieces(w):
    return w.reshape(KB, P, -1, P).transpose(2, 1, 0, 3).reshape(-1, P, PIECE)


def token_pieces(w):
    return w.reshape(KB // 2, 2, P, 512).transpose(0, 2, 1, 3).reshape(-1, P, PIECE)


def kernel(**inputs):
    import concourse.bacc as bacc
    from concourse.bass_utils import run_bass_kernel_spmd

    g = {k: np.asarray(v) for k, v in inputs.items()}
    pieces, cols, rows, sw, ln = [], [], [], [], []

    def column(v):
        return v.reshape(-1, P).T

    for l in range(DEPTH):
        w = g["w_in"][l]
        wo = g["w_out"][l]
        pieces += [token_pieces(g["ada_w"][l][:, c:c + 512]) for c in range(0, 6 * D, 512)]
        pieces += [feature_pieces(w[:, 0:1920][:, 0:896]),
                   feature_pieces(w[:, 896:1920]), token_pieces(w[:, 1920:2432]), feature_pieces(w[:, 2432:3200]),
                   token_pieces(w[:, 3200:3712]), token_pieces(wo[:, 0:512]), token_pieces(wo[:, 512:1024]),
                   feature_pieces(g["peer_wq"][l])]
        cols.append(np.concatenate(
            [column(g["rwkv_conv"][l, j]) for j in range(3)] + [column(g["rwkv_a0"][l])]
            + [column(g["rwkv_w0"][l, d]) for d in range(2)]
            + [column(g[n][l]) for n in ("rwkv_k_k", "rwkv_k_a", "rwkv_r_k", "ada_b")], axis=1))
        rows.append(np.concatenate([g["rwkv_ln_w"][l], g["rwkv_ln_b"][l], g["diff_subln_w"][l], g["hgrn_norm_w"][l],
                                    g["diff_lambda"][l].reshape(-1)]))
        s = np.zeros((P, 512), np.float32)
        s[0:32, 0:256], s[0:32, 256:512] = g["rwkv_w2"][l, 0], g["rwkv_w2"][l, 1]
        s[32:64, 0:256], s[64:128, 0:256] = g["rwkv_a2"][l], g["rwkv_g2"][l]
        sw.append(s)
        ln.append(np.stack([g["ln1_w"][l], g["ln1_b"][l], g["ln2_w"][l], g["ln2_b"][l]]))
    cf, cb = constants()
    arrays = {
        "x": g["x"], "ctx": g["ctx"],
        "cc": np.stack([column(g["c"][0]), column(g["c_ctx"])], axis=2).reshape(P, 2 * KB),
        "cf": cf, "cb": cb, "ws": np.concatenate(pieces), "cols": np.stack(cols), "rows": np.stack(rows),
        "sw": np.stack(sw), "ln": np.stack(ln),
        "sk": g["peer_subkeys"].transpose(0, 3, 1, 2).reshape(DEPTH, P, 2 * NKEYS),
        "lb": np.concatenate([column(g["hgrn_lb_logits"][l]) for l in range(DEPTH)], axis=1),
        "uv": np.concatenate([g["peer_u"], g["peer_v"]], axis=2).reshape(DEPTH * EXPERTS, 2 * D),
    }
    arrays = {k: np.ascontiguousarray(v) for k, v in arrays.items()}
    marks = {}
    for last in range(2):
        nc = bacc.Bacc("TRN2", target_bir_lowering=False, num_devices=1)
        args = {k: nc.dram_tensor(f"in_{k}", v.shape, mybir.dt.from_np(v.dtype), kind="ExternalInput").ap()
                for k, v in arrays.items()}
        args["out"] = nc.dram_tensor("out_x", (1, SEQ, D), F32, kind="ExternalOutput").ap()
        if last:
            marks["real"] = True
        build(nc, args, marks)
    r = run_bass_kernel_spmd(nc, [{f"in_{k}": v for k, v in arrays.items()}], core_ids=[0])
    return r.results[0]["out_x"]
```

```python
import math
from contextlib import ExitStack

import numpy as np
import concourse.bass as bass
from concourse import mybir
from concourse.bass import IndirectOffsetOnAxis

ALU = mybir.AluOpType
ACT = mybir.ActivationFunctionType
AX = mybir.AxisListType
F32 = mybir.dt.float32
U32 = mybir.dt.uint32
I32 = mybir.dt.int32
U8 = mybir.dt.uint8

P = 128
DEPTH, D, SEQ, CTX = 2, 1024, 512, 256
KB = D // P
T = CTX + SEQ
NT = T // P
CT = CTX // P
GRID_W, HD = 64, 64
BH = 4
LEVELS = 7
HEADS, NKEYS, TOPK = 8, 128, 16
EXPERTS = NKEYS * NKEYS
ALPHA = (2.0 * DEPTH) ** 0.25
EPS, GN_EPS, MIN_FORGET = 1e-5, 64e-5, 1e-30
LN_SHIFT = 50
SCALE = HD ** -0.5
WARM = 3
SLOTS = 4
PIECE = 1024
GSLOTS = 8
GROUP = 2
RING = GSLOTS // GROUP
GROUPS = TOPK // GROUP
GSTEP = GROUP + 2
ROUTING = 29
ARENA = 24500
ADA, RW, AQK, AV, HF, HT, WO, WQ = 48, 7, 8, 4, 6, 4, 8, 16
PIECES = ADA + RW + AQK + AV + HF + HT + WO + WQ
C_CONV, C_A0, C_W0, C_KK, C_KA, C_RK, C_ADAB = 0, 18, 20, 24, 26, 28, 30
NCOL = C_ADAB + 48
R_GNW, R_GNB, R_SUB, R_HN, R_LAM = 0, 256, 512, 640, 704
NROW = 960
K_ID, K_ROT, K_ONES, K_BD, K_COS, K_SIN, K_IOTA = 0, 128, 256, 384, 512, 1024, 1536
K_HSEL, K_HALF, K_INV = 1552, 1554, 1556
NCF = K_INV + 2 * LEVELS * P
B_LEV, B_DIAG, B_STRICT, B_INCL = 0, 2 * LEVELS, 2 * LEVELS + 1, 2 * LEVELS + 3
NCB = B_INCL + 2


def orders():
    return [list(range(NT)), list(range(CT))[::-1] + list(range(CT, NT))[::-1]]


class Steps:

    def __init__(self, eng, sem, marks, chained):
        self.eng, self.sem, self.marks, self.chained, self.n = eng, sem, marks, chained, 0

    def __call__(self, ins, *name):
        self.n += 1
        ins.then_inc(self.sem, 1)
        if name:
            self.marks[name] = (self.sem.name, self.n)
        if self.chained:
            self.eng.wait_ge(self.sem, self.n)

    def free(self, ins, *name):
        self.n += 1
        ins.then_inc(self.sem, 1)
        if name:
            self.marks[name] = (self.sem.name, self.n)


def build(nc, a, marks):
    with ExitStack() as ctx:
        def sb(name, n, dt=F32):
            return ctx.enter_context(nc.sbuf_tensor(name, [P, n], dt))

        def sem(name):
            return ctx.enter_context(nc.semaphore(name))

        X = sb("x_tokens", NT * D)
        XT = sb("u_features", KB * T)
        YT = sb("y_features", KB * T)
        CF = sb("consts", NCF)
        CBW = sb("masks", NCB * P // 4, U32)
        CB = CBW[:].bitcast(U8)
        COL = sb("param_cols", NCOL)
        ROW = sb("param_rows", NROW)
        SW = sb("lora_weights", 512)
        SK = sb("subkeys", 2 * NKEYS)
        WR = sb("weight_ring", SLOTS * PIECE)
        MC = sb("mod_cols", 96)
        CC = sb("cond_cols", 2 * KB)
        ST = sb("stats", 64)
        LAM = sb("lambda", 4)
        LB = sb("lower_bounds", 16)
        AR = sb("arena", ARENA)
        PS = ctx.enter_context(nc.psum_tensor("psum", [P, 4096], F32))

        names = ["tensor_steps", "vector_steps", "scalar_steps", "pool_steps", "piece_used", "consts_loaded",
                 "params_loaded", "x_loaded", "ln_rows_loaded", "stored", "ids_staged", "expert_steps", "gelu_done",
                 "diagonals_done", "experts_added", "routing_steps", "heads_placed", "first_scores_kept"]
        SEM = {n: sem(n) for n in names}
        piece_in = [sem(f"piece_in{i}") for i in range(SLOTS)]
        rows_in = [sem(f"rows_in{i}") for i in range(GSLOTS)]

        def at(*name):
            if "real" in marks and name not in marks:
                raise KeyError(name)
            s, n = marks.get(name, ("vector_steps", 1))
            return SEM[s], n

        def bank(b, lo=0, hi=512):
            return PS[:, 512 * b + lo:512 * b + hi]

        def cf(k, n=P):
            return CF[:, k:k + n]

        def mask(i):
            return CB[:, i * P:(i + 1) * P]

        def x_tile(t):
            return X[:, t * D:(t + 1) * D]

        def xt(k, lo=0, hi=T):
            return XT[:, k * T + lo:k * T + hi]

        def yt(k, lo=0, hi=T):
            return YT[:, k * T + lo:k * T + hi]

        def turned(b, t):
            return PS[:, 512 * b + 256 + t * P:512 * b + 256 + (t + 1) * P]

        def rep(ap, n):
            return ap.unsqueeze(1).broadcast_to([P, n, ap.shape[-1]])

        def spread(ap, n):
            return ap.unsqueeze(2).broadcast_to([P, ap.shape[-1], n])

        def split(ap, n):
            return ap.rearrange("p (n c) -> p n c", n=n)

        def runs(ap, lev, second):
            return ap.rearrange("p (n two m) -> p n two m", two=2, m=1 << lev)[:, :, second, :]

        def block_runs(ap, lev, second):
            return ap.rearrange("p b (n two m) -> p b n two m", two=2, m=1 << lev)[:, :, :, second, :]

        def parity_heads(ap):
            return ap.rearrange("p (n two c) -> p two n c", n=2, two=2)

        def parity_banks(b, c):
            return PS[:, 512 * b:512 * b + 1024].rearrange("p (two n) -> p two n", two=2)[:, :, c:c + 256]\
                .rearrange("p two (n c) -> p two n c", n=2)

        def rep4(ap):
            return ap.unsqueeze(1).unsqueeze(1).broadcast_to([P, 2, 2, ap.shape[-1]])

        def tiles(l):
            return list(range(NT)) if l + 1 < DEPTH else list(range(CT, NT))

        ident = cf(K_ID)
        top = [0]

        def take(n):
            v = AR[:, top[0]:top[0] + n]
            top[0] += n
            assert top[0] <= ARENA, top[0]
            return v

        XN = take(NT * D)
        SQ = take(D)
        BC = [take(D) for _ in range(4)]
        LNR = [take(D) for _ in range(2)]
        MR = [take(512)[0:2, :] for _ in range(2)]
        top[0] = 0
        RAW = take(7 * T)
        CV = take(6 * T)
        r_, k_, v_ = (CV[:, n * 2 * T:(n + 1) * 2 * T] for n in range(3))
        nkk, bv, lw0 = (RAW[:, n * 2 * T:(n + 1) * 2 * T] for n in range(3))
        lo_ = RAW[:, 6 * T:7 * T]
        lw1 = YT[:, 6 * T:8 * T]
        RA = YT[:, 2 * T:4 * T]
        VTM = YT[:, 4 * T:6 * T]
        BON = take(24)
        RM = take(48)
        RO = v_
        lw_ = [lw0, lw1]
        rsets = [{n: take(m) for n, m in dict(b=256, ta=256, tb=256, tk=256, tm=768, abT=512, akT=512, qbT=512,
                                              qkT=512, T=512, G=512, X=512, x2=256, w=256, u=256, s=256, sm=256,
                                              bt=2, mc=2).items()} for d in range(2)]
        rtwice = [[{"em": take(2), "tr": YT[:, (2 * d + even) * 256:(2 * d + even + 1) * 256]} for even in range(2)]
                  for d in range(2)]

        def rset(i, d):
            return {**rsets[d], **rtwice[d][i % 2]}

        top[0] = 0
        QA, KA = take(4 * T), take(4 * T)
        VA = take(NT * 512)
        RT = take(SEQ)
        PA = [[take(T) for _ in range(2)] for _ in range(2)]
        PT_ = [take(T) for _ in range(2)]
        OA = take(NT * 512)
        OS = take(NT * 512)
        AST = take(64)
        top[0] = 0
        HQ = take(2 * T)
        HZ = [take(2 * T) for _ in range(2)]
        HK = [take(2 * T) for _ in range(2)]
        HS = take(2 * T)
        HI, HG, HO = take(2 * T), take(2 * T), take(2 * T)
        HM = take(24)
        hsets = [{n: take(m) for n, m in dict(b=256, kh=256, ktm=256, at=512, s=256, bl=2).items()}
                 for d in range(2)]
        htwice = [[{n: take(m) for n, m in dict(dd=LEVELS * 256, el=2).items()} for even in range(2)] for d in range(2)]
        for d in range(2):
            hsets[d]["s1"] = SW[:, d * 256:(d + 1) * 256]
            hsets[d]["eb"] = YT[:, 6 * T + (4 + d) * 256:6 * T + (5 + d) * 256]
            for even in range(2):
                htwice[d][even]["qh"] = YT[:, 6 * T + (2 * d + even) * 256:6 * T + (2 * d + even + 1) * 256]

        def hset(i, d):
            return {**hsets[d], **htwice[d][i % 2]}

        top[0] = 0
        QT = take(16 * T)
        CAND = take(2 * P)
        OH = take(4 * P)
        SV, SIF, CIJF, TOP1 = take(32), take(32), take(32), take(16)
        SI = take(32).bitcast(U32)
        CI = take(16).bitcast(U32)
        CIJ = take(32).bitcast(U32)
        E0 = take(32)
        TOP = take(P)
        GS = take(2 * HEADS)
        GATE = [take(P) for _ in range(2)]
        IDX = [take(P).bitcast(U32) for _ in range(2)]
        DOT, GEL, WGT = take(8), take(8), take(8)
        IDS = take(8).bitcast(U32)
        DUM, DUM_DVE = take(1), take(1)
        U2 = YT
        GB = [XT[:, i * 2048:(i + 1) * 2048] for i in range(3)] + [take(2048) for i in range(5)]
        ACC, ACC_PE = PS[:, 0:D], PS[:, 3072:3072 + D]
        DIAG = [SW[:, i * P:(i + 1) * P] for i in range(RING)]

        def gate2_row(s):
            return PS[:, 1024 * (s + 1):1024 * (s + 1) + D]

        def score_cols(t):
            return split(QT, 16)[:, :, t * P:(t + 1) * P]

        LNR2 = [score_cols(0)[:, 0:KB, :], score_cols(0)[:, KB:, :]]
        SQ2 = score_cols(1)[:, 0:KB, :]
        MIX = score_cols(1)[:, KB:, :]

        block = ctx.enter_context(nc.Block())

        @block.sync
        def _(sp):
            sp.dma_start(CF[:], a["cf"]).then_inc(SEM["consts_loaded"], 16)
            sp.dma_start(CBW[:], a["cb"]).then_inc(SEM["consts_loaded"], 16)
            sp.dma_start(CC[:], a["cc"]).then_inc(SEM["consts_loaded"], 16)
            xv = X[:].rearrange("p (t n) -> p t n", t=NT)
            sp.dma_start(xv[:, 0:CT, :], a["ctx"].rearrange("b (t p) n -> p (b t) n", p=P)).then_inc(SEM["x_loaded"], 16)
            sp.dma_start(xv[:, CT:NT, :], a["x"].rearrange("b (t p) n -> p (b t) n", p=P)).then_inc(SEM["x_loaded"], 16)
            total = DEPTH * PIECES
            for j in range(SLOTS):
                sp.dma_start(WR[:, j * PIECE:(j + 1) * PIECE], a["ws"][j]).then_inc(piece_in[j], 16)
            with sp.Fori(1, total // SLOTS) as i:
                for j in range(SLOTS):
                    sp.wait_ge(SEM["piece_used"], i * SLOTS + (j + 1 - SLOTS))
                    sp.dma_start(WR[:, j * PIECE:(j + 1) * PIECE],
                                 a["ws"][bass.ds(i * SLOTS + j, 1)].rearrange("a p n -> p (a n)")).then_inc(piece_in[j], 16)
            for n in range(total // SLOTS * SLOTS, total):
                j = n % SLOTS
                sp.wait_ge(SEM["piece_used"], n + 1 - SLOTS)
                sp.dma_start(WR[:, j * PIECE:(j + 1) * PIECE], a["ws"][n]).then_inc(piece_in[j], 16)
            sp.wait_ge(*at("final", DEPTH - 1, NT - 1))
            sp.dma_start(a["out"].rearrange("b (t p) n -> p (b t) n", p=P), xv[:, CT:NT, :]).then_inc(SEM["stored"], 16)
            sp.wait_ge(SEM["stored"], 16)

        @block.tensor
        def _(pe):
            done = Steps(pe, SEM["tensor_steps"], marks, False)
            piece = [0]

            def mm(o, w, x, first=True, last=True):
                return pe.matmul(o, w, x, start=first, stop=last, skip_group_check=True)

            def keep_warm(o, n):
                for _ in range(n):
                    mm(o, ident, ident)

            def piece_ready():
                n = piece[0]
                pe.wait_ge(piece_in[n % SLOTS], 16 * (n // SLOTS + 1))
                return WR[:, (n % SLOTS) * PIECE:(n % SLOTS + 1) * PIECE]

            def piece_done(ins, *name):
                piece[0] += 1
                ins.then_inc(SEM["piece_used"], 1)
                if name:
                    marks[name] = ("piece_used", piece[0])

            def first_scores(l, h):
                t = tiles(l)[0]
                pe.wait_ge(*at("peer copied", l, 2 * h + 1))
                if h >= 2:
                    pe.wait_ge(SEM["first_scores_kept"], l * HEADS + h - 1)
                for j in range(2):
                    c = (2 * h + j) * T + t * P
                    ins = mm(bank(4 + h % 2, j * P, (j + 1) * P), QT[:, c:c + P], SK[:, j * P:(j + 1) * P])
                done(ins, "first scores", l, h)

            def project(l, what, count):
                for c in range(count):
                    w = piece_ready()
                    if c >= 2:
                        pe.wait_ge(*at(what + " copied", l, c - 2))
                    p0 = 2 * (c % 2)
                    for o, lo, hi in ((bank(p0, 256, 512), 0, CTX), (bank(p0 + 1), CTX, T)):
                        for k in range(KB):
                            ins = mm(o, w[:, k * P:(k + 1) * P], xt(k, lo, hi), k == 0, k == KB - 1)
                    piece_done(ins, what + " projected", l, c)
                    if what == "peer" and c >= 2 and c % 2 == 0:
                        first_scores(l, c // 2 - 1)

            def project_tokens(what, src, ts, *name):
                for c in range(KB // 2):
                    w = piece_ready()
                    for n, t in enumerate(ts):
                        for k in range(2):
                            ins = mm(bank(n), src(2 * c + k, t * P, (t + 1) * P), w[:, k * 512:(k + 1) * 512],
                                     c == 0 and k == 0, c == KB // 2 - 1 and k == 1)
                    piece_done(ins, *(name if c == KB // 2 - 1 else ()))

            def transpose_x(l, what, ts):
                for k in range(KB):
                    if k >= 3:
                        pe.wait_ge(*at(what + " modulated", l, k - 3))
                    for t in ts:
                        if k == 0:
                            pe.wait_ge(*at(what + " normed", l, t))
                        ins = pe.transpose(turned(2 * (k % 3), t), XN[:, t * D + k * P:t * D + (k + 1) * P], ident)
                    done(ins, what + " turned", l, k)

            def broadcast(l, what, firsts, streams):
                for n, s in enumerate(streams):
                    if n:
                        pe.wait_ge(*at(what + " kept", l, streams[0]))
                    for v, first in enumerate(firsts):
                        for k in range(KB):
                            j = 2 * (first + k) + s
                            ins = mm(bank(2 * v + k // 4, (k % 4) * P, (k % 4 + 1) * P),
                                     MC[:, j:j + 1].broadcast_to([P, P]), ident)
                    done(ins, what + " rows", l, s)

            def by_parity(b, h, c):
                return bank(b + h % 2, c + h // 2 * P, c + (h // 2 + 1) * P)

            def head_rows(h):
                return slice(64 * (h % 2), 64 * (h % 2) + 64)

            def block_cols(h):
                return slice((h // 2) * P, (h // 2 + 1) * P)

            pe.wait_ge(SEM["consts_loaded"], 48)
            for l in range(DEPTH):
                streams = [0, 1] if l + 1 < DEPTH else [0]
                if l == 0:
                    pe.wait_ge(*at("cond silu"))
                else:
                    pe.wait_ge(*at("final", l - 1, NT - 1))
                for c in range(ADA // 4 + 1):
                    if c < ADA // 4:
                        if c >= 2:
                            pe.wait_ge(*at("ada rows kept", l, c - 2))
                        for n in range(4):
                            w = piece_ready()
                            for j in range(2):
                                k = 2 * n + j
                                ins = mm(bank(5 + 2 * (c % 2))[0:2, :], CC[:, 2 * k:2 * k + 2], w[:, j * 512:(j + 1) * 512],
                                         k == 0, k == KB - 1)
                            piece_done(ins, "ada rows", l, c)
                    if c:
                        pe.wait_ge(*at("ada rows kept", l, c - 1))
                        for j in range(4):
                            n = 4 * (c - 1) + j
                            ins = mm(bank(6, 2 * n, 2 * n + 2), MR[(c - 1) % 2][:, j * P:(j + 1) * P], ident[0:2, 0:2])
                        done(ins, "ada turned", l, c - 1)
                transpose_x(l, "ln1", range(NT))
                pe.wait_ge(*at("ln1 modulated", l, KB - 1))
                project(l, "rwkv", RW)
                pe.wait_ge(*at("rwkv kk squared", l))
                for b in range(2):
                    pe.wait_ge(*at("rwkv copied", l, RW - 1))
                    mm(bank(2 * b, 256, 512), cf(K_BD), bv[:, b * T:b * T + CTX])
                    done(mm(bank(2 * b + 1), cf(K_BD), bv[:, b * T + CTX:(b + 1) * T]), "rwkv kk norm", l, b)
                pe.wait_ge(*at("rwkv lora in", l))
                for j in range(6):
                    rows = slice(32, 64) if j < 2 else slice(0, 32)
                    c0 = 256 if j >= 4 else 0
                    if j < 2:
                        pe.wait_ge(*at("rwkv kk floored", l, j))
                    if j >= 3:
                        pe.wait_ge(*at("rwkv gate read", l, j - 3))
                    w = SW[rows, c0 + (j % 2) * P:c0 + (j % 2 + 1) * P]
                    mm(bank(2 * (j % 3), 256, 512), w, lo_[rows, 0:CTX])
                    done(mm(bank(2 * (j % 3) + 1), w, lo_[rows, CTX:T]), "rwkv gate", l, j)
                for j in (3, 4, 5):
                    pe.wait_ge(*at("rwkv gate read", l, j))
                for t in range(NT):
                    for b in range(2):
                        c = t * 256 + b * P
                        ins = pe.transpose(PS[:, c:c + P], v_[:, b * T + t * P:b * T + (t + 1) * P], ident)
                done(ins, "rwkv v turned", l)
                pe.wait_ge(*at("rwkv gate read", l, 5))
                pe.wait_ge(*at("rwkv rk", l))
                for t in range(NT):
                    for b in range(2):
                        ins = mm(bank(7, t * 4 + 2 * b, t * 4 + 2 * b + 2), RA[:, b * T + t * P:b * T + (t + 1) * P],
                                 cf(K_HSEL, 2))
                done(ins, "rwkv bonus", l)
                pe.wait_ge(*at("rwkv ready", l))
                pe.wait_ge(*at("rwkv v kept", l))
                for i in range(NT):
                    R = [(d, orders()[d][i], rset(i, d), 4 * d) for d in range(2)]
                    for d, t, q, b0 in R:
                        if i:
                            pe.wait_ge(*at("rwkv U kept", l, i - 1, d))
                        pe.wait_ge(*at("rwkv scaled", l, i, d))
                        for n, src in enumerate(("ta", "tb", "tk")):
                            for b in range(2):
                                c = 512 * b0 + (2 * n + b) * P
                                ins = pe.transpose(PS[:, c:c + P], q[src][:, b * P:(b + 1) * P], ident)
                        done(ins, "rwkv abk turned", l, i, d)
                    for d, t, q, b0 in R:
                        pe.wait_ge(*at("rwkv abk kept", l, i, d))
                        if i:
                            pe.wait_ge(*at("rwkv state", l, i - 1, d))
                        for n, (s, m) in enumerate((("tb", "ta"), ("tk", "ta"), ("tb", "tr"), ("tk", "tr"))):
                            for h in range(4):
                                ins = mm(by_parity(b0 + n // 2 * 2, h, n % 2 * 256), q[s][head_rows(h), block_cols(h)],
                                         q[m][head_rows(h), block_cols(h)])
                            done(ins, "rwkv scores", l, i, d, n)
                    for lev in range(LEVELS):
                        for d, t, q, b0 in R:
                            if lev == 0:
                                pe.wait_ge(*at("rwkv scores kept", l, i, d))
                            else:
                                pe.wait_ge(*at("rwkv T", l, i, d, lev - 1))
                            for h in range(4):
                                c = slice(h * P, (h + 1) * P)
                                if lev == 0:
                                    ins = mm(by_parity(b0, h, 0), q["ta"][head_rows(h), block_cols(h)],
                                             q["tb"][head_rows(h), block_cols(h)])
                                elif lev == 1:
                                    ins = mm(bank(b0, h * P, (h + 1) * P), q["abT"][:, c], q["T"][:, c])
                                else:
                                    left = d
                                    ins = mm(runs(bank(b0, h * P, (h + 1) * P), lev, left), q["abT"][:, c],
                                             runs(q["T"][:, c], lev, left))
                            done(ins, "rwkv AT", l, i, d, lev)
                        keep_warm(bank(3, 0, P), WARM)
                        for d, t, q, b0 in R:
                            pe.wait_ge(*at("rwkv X", l, i, d, lev))
                            left, right = (0, 1) if d == 0 else (1, 0)
                            for h in range(4):
                                c = slice(h * P, (h + 1) * P)
                                G = ident if lev == 0 else q["G"][:, c]
                                if 0 < lev < LEVELS - 1:
                                    mm(runs(bank(b0 + 1, h * P, (h + 1) * P), lev, left), G, runs(q["X"][:, c], lev, left))
                                ins = mm(runs(bank(b0 + 2, h * P, (h + 1) * P), lev, right), q["X"][:, c],
                                         runs(G, lev, right))
                            done(ins, "rwkv dT", l, i, d, lev)
                        keep_warm(bank(3, 0, P), WARM)
                    for d, t, q, b0 in R:
                        pe.wait_ge(*at("rwkv G", l, i, d, LEVELS - 1))
                        for h in range(4):
                            mm(bank(b0 + 3, h * 64, h * 64 + 64), q["akT"][:, h * P:(h + 1) * P],
                               VTM[:, t * 256 + h * 64:t * 256 + h * 64 + 64])
                            c = 512 * b0 + (h // 2) * P
                            ins = mm(PS[head_rows(h), c:c + P], q["tm"][:, h * 64:h * 64 + 64], q["G"][:, h * P:(h + 1) * P])
                        done(ins, "rwkv W", l, i, d)
                    for d, t, q, b0 in R:
                        pe.wait_ge(*at("rwkv W kept", l, i, d))
                        pe.wait_ge(*at("rwkv state scaled", l, i, d))
                        for b in range(2):
                            mm(bank(b0 + 1, b * P, (b + 1) * P), q["w"][:, b * P:(b + 1) * P],
                               q["sm"][:, b * P:(b + 1) * P], True, False)
                            for h in (2 * b, 2 * b + 1):
                                ins = mm(bank(b0 + 1, h * 64, h * 64 + 64), q["G"][:, h * P:(h + 1) * P],
                                         q["x2"][:, h * 64:h * 64 + 64], False, True)
                        done(ins, "rwkv U", l, i, d)
                    for d, t, q, b0 in R:
                        pe.wait_ge(*at("rwkv U kept", l, i, d))
                        for b in range(2):
                            c = slice(b * P, (b + 1) * P)
                            o = bank(b0 + 3, 256 + b * P, 256 + (b + 1) * P)
                            mm(o, q["tm"][:, 256 + b * P:256 + (b + 1) * P], q["u"][:, c], True, False)
                            mm(o, q["tm"][:, 512 + b * P:512 + (b + 1) * P],
                               VTM[:, t * 256 + b * P:t * 256 + (b + 1) * P], False, True)
                        for b in range(2):
                            c = slice(b * P, (b + 1) * P)
                            mm(bank(b0 + 2, b * P, (b + 1) * P), q["tr"][:, c], q["sm"][:, c], True, False)
                            for h in (2 * b, 2 * b + 1):
                                o = bank(b0 + 2, h * 64, h * 64 + 64)
                                mm(o, q["qbT"][:, h * P:(h + 1) * P], q["u"][:, h * 64:h * 64 + 64], False, False)
                                ins = mm(o, q["qkT"][:, h * P:(h + 1) * P],
                                         VTM[:, t * 256 + h * 64:t * 256 + h * 64 + 64], False, True)
                        done(ins, "rwkv out", l, i, d)
                for d in range(2):
                    pe.wait_ge(*at("rwkv state", l, NT - 1, d))
                for t in range(NT):
                    ins = mm(PS[:, t * 256:(t + 1) * 256], lo_[64:128, t * P:(t + 1) * P], SW[64:128, 0:256])
                done(ins, "rwkv g", l)
                pe.wait_ge(*at("rwkv y", l))
                for b in range(2):
                    for t in tiles(l):
                        ins = pe.transpose(turned(2 * b, t), RO[:, t * 256 + b * P:t * 256 + (b + 1) * P], ident)
                done(ins, "rwkv y turned", l)
                pe.wait_ge(*at("rwkv y features", l))
                project(l, "attn", AQK)
                pe.wait_ge(*at("attn copied", l, AQK - 1))
                project_tokens("attn", xt, range(NT), "attn v", l)
                for n in range(8):
                    if n >= 2:
                        pe.wait_ge(*at("rope", l, n - 2))
                    src = QA if n < 4 else KA
                    done(mm(bank(6 + n % 2), cf(K_ROT), src[:, (n % 4) * T + CTX:(n % 4 + 1) * T]), "rotated", l, n)
                pe.wait_ge(*at("rope", l, 7))
                pe.wait_ge(*at("attn v kept", l))
                jobs = [(t, h) for t in tiles(l) for h in range(BH)]
                for n in range(len(jobs) + 2):
                    if n < len(jobs):
                        t, h = jobs[n]
                        for m in range(2):
                            if n:
                                pe.wait_ge(*at("attn exp", l, n - 1, m))
                            rows = slice(64 * m, 64 * m + 64)
                            q = QA[rows, h * T + t * P:h * T + (t + 1) * P]
                            ins = mm(bank(2 * m, 256, 512), q, KA[rows, h * T:h * T + CTX])
                            if t >= CT:
                                ins = mm(bank(2 * m + 1), q, KA[rows, h * T + CTX:(h + 1) * T])
                            done(ins, "attn scores", l, n, m)
                    if 1 <= n <= len(jobs):
                        j = n - 1
                        nk = NT if jobs[j][0] >= CT else CT
                        pe.wait_ge(*at("attn a", l, j))
                        if j:
                            pe.wait_ge(*at("attn aT", l, j - 1))
                        for k in range(nk):
                            ins = pe.transpose(PS[:, 2048 + k * P:2048 + (k + 1) * P], PA[j % 2][0][:, k * P:(k + 1) * P], ident)
                        done(ins, "attn a turned", l, j)
                    if n >= 2:
                        j = n - 2
                        t, h = jobs[j]
                        nk = NT if t >= CT else CT
                        pe.wait_ge(*at("attn aT", l, j))
                        if j:
                            pe.wait_ge(*at("attn o", l, j - 1))
                        for k in range(nk):
                            ins = mm(bank(6, 0, P), PT_[j % 2][:, k * P:(k + 1) * P],
                                     VA[:, k * 512 + h * P:k * 512 + (h + 1) * P], k == 0, k == nk - 1)
                        done(ins, "attn pv", l, j)
                pe.wait_ge(*at("attn y", l))
                for h in range(BH):
                    for t in tiles(l):
                        ins = pe.transpose(turned(2 * h, t), OA[:, t * 512 + h * P:t * 512 + (h + 1) * P], ident)
                    done(ins, "attn y turned", l, h)
                pe.wait_ge(*at("attn y features", l, BH - 1))
                project(l, "hgrn", HF)
                pe.wait_ge(*at("hgrn copied", l, HF - 1))
                project_tokens("hgrn", xt, range(NT), "hgrn ig", l)
                pe.wait_ge(*at("hgrn ig kept", l))
                pe.wait_ge(*at("hgrn ready", l))
                for i in range(NT):
                    R = [(d, orders()[d][i], hset(i, d), 4 * d) for d in range(2)]
                    for d, t, q, b0 in R:
                        if i:
                            pe.wait_ge(*at("hgrn state", l, i - 1, d))
                        pe.wait_ge(*at("hgrn scaled", l, i, d))
                        for b in range(2):
                            ins = pe.transpose(bank(b0, b * P, (b + 1) * P), q["kh"][:, b * P:(b + 1) * P], ident)
                        done(ins, "hgrn k turned", l, i, d)
                    for n in range(LEVELS + 1):
                        for d, t, q, b0 in R:
                            if n >= 2:
                                pe.wait_ge(*at("hgrn placed", l, i, d, n - 2))
                            if n == 0:
                                pe.wait_ge(*at("hgrn k kept", l, i, d))
                            if n == 1:
                                pe.wait_ge(*at("hgrn pairs", l, i, d))
                            keep_warm(bank(b0 + 2 * (n % 2), 256, 384), 1)
                            for h in range(4):
                                rows = head_rows(h)
                                o = by_parity(b0 + 2 * (n % 2), h, 256)
                                c = (h // 2) * T + t * P
                                if n == 0:
                                    ins = mm(o, HK[d][rows, c:c + P], HQ[rows, c:c + P])
                                else:
                                    f = q["dd"][rows, (n - 1) * 256 + (h // 2) * P:(n - 1) * 256 + (h // 2 + 1) * P]
                                    ins = mm(runs(o, n - 1, 1 - d), f, runs(f, n - 1, 1 - d))
                            done(ins, "hgrn level", l, i, d, n)
                    for d, t, q, b0 in R:
                        pe.wait_ge(*at("hgrn placed", l, i, d, LEVELS))
                        for b in range(2):
                            c = slice(b * P, (b + 1) * P)
                            mm(bank(b0 + 2, b * P, (b + 1) * P), q["ktm"][:, c], HI[:, t * 256 + b * P:t * 256 + (b + 1) * P])
                        for b in range(2):
                            c = slice(b * P, (b + 1) * P)
                            mm(bank(b0 + 1, b * P, (b + 1) * P), q["qh"][:, c], q["s"][:, c], True, False)
                            for h in (2 * b, 2 * b + 1):
                                ins = mm(bank(b0 + 1, h * 64, h * 64 + 64), q["at"][:, h * P:(h + 1) * P],
                                         HI[:, t * 256 + h * 64:t * 256 + h * 64 + 64], False, True)
                        done(ins, "hgrn out", l, i, d)
                pe.wait_ge(*at("hgrn y", l))
                for b in range(2):
                    for t in tiles(l):
                        ins = pe.transpose(turned(2 * b, t), HO[:, t * 256 + b * P:t * 256 + (b + 1) * P], ident)
                done(ins, "hgrn y turned", l)
                pe.wait_ge(*at("hgrn y features", l))
                broadcast(l, "gate1", [16], streams)
                pe.wait_ge(*at("gate1 kept", l, streams[-1]))
                for half in range(2):
                    if half:
                        pe.wait_ge(*at("mixed", l, 0))
                    project_tokens("out", yt, tiles(l), "out projected", l, half)
                pe.wait_ge(*at("mixed", l, 1))
                broadcast(l, "mod2", [24, 32], streams)
                pe.wait_ge(*at("mod2 kept", l, streams[-1]))
                transpose_x(l, "ln2", tiles(l))
                pe.wait_ge(*at("ln2 modulated", l, KB - 1))
                project(l, "peer", WQ)
                first_scores(l, HEADS - 1)
                pe.wait_ge(SEM["first_scores_kept"], (l + 1) * HEADS)
                for n, t in enumerate(tiles(l)[1:]):
                    if n >= 2:
                        pe.wait_ge(*at("peer scores kept", l, t - 2))
                    for j in range(2 * HEADS):
                        ins = mm(bank(4 * (n % 2) + j // 4, (j % 4) * P, (j % 4 + 1) * P),
                                 QT[:, j * T + t * P:j * T + (t + 1) * P], SK[:, (j % 2) * P:(j % 2 + 1) * P])
                    done(ins, "peer scores", l, t)
                for t in tiles(l)[-2:]:
                    pe.wait_ge(*at("peer scores kept", l, t))
                for s in streams:
                    for k in range(KB):
                        j = 2 * (40 + k) + s
                        ins = mm(gate2_row(s)[:, k * P:(k + 1) * P], MC[:, j:j + 1].broadcast_to([P, P]), ident)
                done(ins, "gate2 rows", l)
                for n, t in enumerate(tiles(l)):
                    base = (l * NT + n) * HEADS
                    if n:
                        pe.wait_ge(*at("sums taken", l, t - 1))
                    for c in range(2):
                        ins = mm(ACC_PE[:, c * 512:(c + 1) * 512], cf(K_INV)[0:1, :], cf(K_COS, 512)[0:1, :], True, False)
                    if l == 0 and n == 0:
                        ins.then_inc(SEM["experts_added"], RING - 1)
                    with pe.Fori(0, HEADS) as i:
                        for g in range(GROUPS):
                            pe.wait_ge(SEM["diagonals_done"], (i + base) * GROUPS + (g + 1))
                            v = GB[g % RING * GROUP + 1]
                            for c in range(2):
                                ins = mm(ACC_PE[:, c * 512:(c + 1) * 512], DIAG[g % RING],
                                         v[:, D + c * 512:D + (c + 1) * 512], False, False)
                            ins.then_inc(SEM["experts_added"], 1)

        @block.scalar
        def _(act):
            done = Steps(act, SEM["scalar_steps"], marks, True)
            params = [0]

            def load(dst, src):
                act.dma_start(dst, src).then_inc(SEM["params_loaded"], 16)
                params[0] += 16

            def copy(o, i, *name):
                done(act.activation(o, i, ACT.Copy), *name)

            def pair(b, lo=0):
                return PS[:, 512 * b + 256 + lo:512 * b + 1024]

            def stats(l, what, ts, sq, n=1):
                for t in ts:
                    if what != "ln1":
                        act.wait_ge(*at(what + " input", l, t))
                    done(act.activation(sq, split(x_tile(t), n) if n > 1 else x_tile(t), ACT.Copy, accum_out=ST[:, t:t + 1]), what + " sum", l, t)
                for t in ts:
                    act.wait_ge(*at(what + " mean", l, t))
                    done(act.activation(sq, split(x_tile(t), n) if n > 1 else x_tile(t), ACT.Square, bias=ST[:, 8 + t:9 + t],
                                        accum_out=ST[:, 16 + t:17 + t]), what + " squares", l, t)

            def rwkv_decays(l, i):
                for d in range(2):
                    q = rset(i, d)
                    act.wait_ge(*at("rwkv centred", l, i, d))
                    done.free(act.activation(q["em"], q["bt"], ACT.Exp, scale=0.5))
                    done.free(act.activation(q["tr"], q["b"], ACT.Exp))
                    done.free(act.activation(q["tk"], q["b"], ACT.Exp, scale=-1.0))
                    done(act.activation(q["ta"], q["ta"], ACT.Exp), "rwkv decays", l, i, d)

            def hgrn_decays(l, i):
                for d in range(2):
                    q = hset(i, d)
                    act.wait_ge(*at("hgrn sums", l, i, d))
                    done.free(act.activation(q["eb"], q["b"], ACT.Exp))
                    done.free(act.activation(q["el"], q["bl"], ACT.Exp))
                    done(act.activation(q["kh"], q["kh"], ACT.Exp), "hgrn decays", l, i, d)
                    act.wait_ge(*at("hgrn differences", l, i, d))
                    done(act.activation(q["dd"], q["dd"], ACT.Abs))
                    done(act.activation(q["dd"], q["dd"], ACT.Exp, scale=-1.0), "hgrn level decays", l, i, d)

            def first_scores(l, h):
                act.wait_ge(*at("first scores", l, h))
                act.activation(score_cols(tiles(l)[0])[:, 2 * h:2 * h + 2, :], split(bank(4 + h % 2, 0, 256), 2),
                               ACT.Copy).then_inc(SEM["first_scores_kept"], 1)

            def rows_kept(l, what, dsts, streams):
                for s in streams:
                    act.wait_ge(*at(what + " rows", l, s))
                    for n, dst in enumerate(dsts(s)):
                        copy(dst, PS[:, 1024 * n:1024 * n + D])
                    marks[(what + " kept", l, s)] = (SEM["scalar_steps"].name, done.n)

            act.wait_ge(SEM["consts_loaded"], 48)
            done(act.activation(ST[:, 32:48], CC[:], ACT.Sigmoid), "cond sigmoid")
            act.wait_ge(SEM["x_loaded"], 32)
            for l in range(DEPTH):
                streams = [0, 1] if l + 1 < DEPTH else [0]
                ts = tiles(l)
                if l:
                    act.wait_ge(*at("final", l - 1, NT - 1))
                load(COL[:], a["cols"][l])
                load(ROW[:], a["rows"][l].partition_broadcast(P))
                load(SW[:], a["sw"][l])
                load(SK[:], a["sk"][l])
                if l == 0:
                    load(LB[:, 0:4], a["lb"])
                marks[("params", l)] = ("params_loaded", params[0])
                stats(l, "ln1", range(NT), SQ)
                for c in range(ADA // 4):
                    act.wait_ge(*at("ada rows", l, c))
                    if c >= 2:
                        act.wait_ge(*at("ada turned", l, c - 2))
                    copy(MR[c % 2], bank(5 + 2 * (c % 2))[0:2, :], "ada rows kept", l, c)
                act.wait_ge(*at("lambda sums", l))
                done(act.activation(LAM[:, 0:2], LAM[:, 0:2], ACT.Exp), "lambda exp", l)
                if l == 0:
                    act.wait_ge(*at("bounds shifted"))
                    done(act.activation(LB[:, 4:8], LB[:, 4:8], ACT.Exp), "bounds exp")
                act.wait_ge(*at("ln1 modulated", l, KB - 1))
                for c in range(RW):
                    act.wait_ge(*at("rwkv projected", l, c))
                    copy(RAW[:, c * T:(c + 1) * T], pair(2 * (c % 2)), "rwkv copied", l, c)
                done(act.activation(lo_[0:32, :], lo_[0:32, :], ACT.Tanh))
                done(act.activation(lo_[64:128, :], lo_[64:128, :], ACT.Sigmoid), "rwkv lora in", l)
                act.wait_ge(*at("rwkv conv", l))
                for b in range(2):
                    act.wait_ge(*at("rwkv kk floored", l, b))
                    done(act.activation(bv[:, b * T:(b + 1) * T], bv[:, b * T:(b + 1) * T], ACT.Sqrt), "rwkv kk root", l, b)
                for j in range(6):
                    act.wait_ge(*at("rwkv gate", l, j))
                    dst = (RA, lw0, lw1)[j // 2][:, (j % 2) * T:(j % 2 + 1) * T]
                    bias = COL[:, C_A0 + j:C_A0 + j + 1]
                    done(act.activation(dst, pair(2 * (j % 3)), ACT.Sigmoid, bias=bias), "rwkv gate read", l, j)
                act.wait_ge(*at("rwkv v turned", l))
                copy(VTM, PS[:, 0:2 * T], "rwkv v kept", l)
                rwkv_decays(l, 0)
                for i in range(NT):
                    R = [(d, orders()[d][i], rset(i, d), 4 * d) for d in range(2)]
                    for d, t, q, b0 in R:
                        act.wait_ge(*at("rwkv abk turned", l, i, d))
                        copy(q["tm"], PS[:, 512 * b0:512 * b0 + 768], "rwkv abk kept", l, i, d)
                    if i + 1 < NT:
                        rwkv_decays(l, i + 1)
                    for d, t, q, b0 in R:
                        act.wait_ge(*at("rwkv W", l, i, d))
                        copy(q["x2"], bank(b0 + 3, 0, 256))
                        copy(q["w"], bank(b0, 0, 256), "rwkv W kept", l, i, d)
                    for d, t, q, b0 in R:
                        act.wait_ge(*at("rwkv U", l, i, d))
                        copy(q["u"], bank(b0 + 1, 0, 256), "rwkv U kept", l, i, d)
                act.wait_ge(*at("rwkv y turned", l))
                lo = 0 if l + 1 < DEPTH else CTX
                copy(yt(0, lo), pair(0, lo))
                copy(yt(1, lo), pair(2, lo), "rwkv y features", l)
                for c in range(AQK):
                    act.wait_ge(*at("attn projected", l, c))
                    copy((QA if c < 4 else KA)[:, (c % 4) * T:(c % 4 + 1) * T], pair(2 * (c % 2)), "attn copied", l, c)
                act.wait_ge(*at("attn v", l))
                copy(VA, PS[:, 0:NT * 512], "attn v kept", l)
                jobs = [(t, h) for t in ts for h in range(BH)]
                for n in range(len(jobs) + 1):
                    if n < len(jobs):
                        keys = T if jobs[n][0] >= CT else CTX
                        c0 = 16 * (n % 2)
                        for m in range(2):
                            act.wait_ge(*at("attn max", l, n, m))
                            if m == 0 and n >= 2:
                                act.wait_ge(*at("attn a turned", l, n - 2))
                            done(act.activation(PA[n % 2][m][:, 0:keys], PS[:, 1024 * m + 256:1024 * m + 256 + keys], ACT.Exp,
                                                bias=AST[:, c0 + 2 + m:c0 + 3 + m], scale=SCALE,
                                                accum_out=AST[:, c0 + 4 + m:c0 + 5 + m]), "attn exp", l, n, m)
                    if n:
                        keys = T if jobs[n - 1][0] >= CT else CTX
                        act.wait_ge(*at("attn a turned", l, n - 1))
                        if n >= 3:
                            act.wait_ge(*at("attn pv", l, n - 3))
                        copy(PT_[(n - 1) % 2][:, 0:keys], PS[:, 2048:2048 + keys], "attn aT", l, n - 1)
                for h in range(BH):
                    act.wait_ge(*at("attn y turned", l, h))
                    copy(yt(2 + h, lo), pair(2 * h, lo), "attn y features", l, h)
                for c in range(HF):
                    act.wait_ge(*at("hgrn projected", l, c))
                    copy(AR[:, c * T:(c + 1) * T], pair(2 * (c % 2)), "hgrn copied", l, c)
                act.wait_ge(*at("hgrn ig", l))
                ig = PS[:, 0:NT * 512].rearrange("p (t two c) -> p t two c", t=NT, two=2)
                copy(split(HI, NT), ig[:, :, 0, :])
                copy(split(HG, NT), ig[:, :, 1, :], "hgrn ig kept", l)
                done(act.activation(HS, HQ, ACT.Sigmoid), "hgrn q gate", l)
                for d in range(2):
                    done(act.activation(HK[d], HZ[d], ACT.Sigmoid, scale=-1.0))
                    done(act.activation(HZ[d], HZ[d], ACT.Sigmoid), "hgrn gates", l, d)
                for d in range(2):
                    act.wait_ge(*at("hgrn f", l, d))
                    done(act.activation(HZ[d], HZ[d], ACT.Ln), "hgrn log", l, d)
                hgrn_decays(l, 0)
                for i in range(NT):
                    R = [(d, orders()[d][i], hset(i, d), 4 * d) for d in range(2)]
                    for d, t, q, b0 in R:
                        act.wait_ge(*at("hgrn k turned", l, i, d))
                        copy(q["ktm"], bank(b0, 0, 256), "hgrn k kept", l, i, d)
                    if i + 1 < NT:
                        hgrn_decays(l, i + 1)
                done(act.activation(HS, HG, ACT.Sigmoid), "hgrn g gate", l)
                act.wait_ge(*at("hgrn y turned", l))
                copy(yt(6, lo), pair(0, lo))
                copy(yt(7, lo), pair(2, lo), "hgrn y features", l)
                act.dma_start(LNR[0], a["ln"][l, 0].partition_broadcast(P)).then_inc(SEM["ln_rows_loaded"], 16)
                act.dma_start(LNR[1], a["ln"][l, 1].partition_broadcast(P)).then_inc(SEM["ln_rows_loaded"], 16)
                rows_kept(l, "gate1", lambda s: [BC[s]], streams)
                stats(l, "mix", ts, SQ)
                act.wait_ge(*at("mixed", l, 1))
                rows_kept(l, "mod2", lambda s: [BC[2 * s], BC[2 * s + 1]], streams)
                stats(l, "ln2", ts, SQ)
                act.wait_ge(*at("peer input", l))
                for c in range(WQ):
                    act.wait_ge(*at("peer projected", l, c))
                    copy(QT[:, c * T + lo:(c + 1) * T], pair(2 * (c % 2), lo), "peer copied", l, c)
                    if c >= 3 and c % 2:
                        first_scores(l, c // 2 - 1)
                first_scores(l, HEADS - 1)
                for n, t in enumerate(ts[1:]):
                    act.wait_ge(*at("peer scores", l, t))
                    copy(score_cols(t), split(PS[:, 2048 * (n % 2):2048 * (n % 2) + 2048], 16), "peer scores kept", l, t)
                act.wait_ge(*at("peer centred", l, ts[0]))
                done(act.activation(TOP, TOP, ACT.Exp), "peer exp", l, ts[0])
                act.wait_ge(*at("routed", l, ts[0]))
                for j in range(2):
                    act.dma_start(LNR2[j], split(a["ln"][l, 2 + j].partition_broadcast(P), KB)).then_inc(SEM["ln_rows_loaded"], 16)
                for n, t in enumerate(ts):
                    base = (l * NT + n) * HEADS
                    with act.Fori(0, HEADS) as i:
                        for g in range(GROUPS):
                            c = g % RING * GROUP
                            now = ((i + base) * GROUPS + (g + RING - 1)) * GSTEP
                            act.wait_ge(SEM["expert_steps"], now + GROUP)
                            act.activation(GEL[:, c:c + GROUP], DOT[:, c:c + GROUP], ACT.Gelu).then_inc(SEM["gelu_done"], 1)
                            act.wait_ge(SEM["expert_steps"], now + (GROUP + 1))
                            act.activation(DIAG[g % RING], ident, ACT.Copy, scale=WGT[:, c + 1:c + 2])\
                                .then_inc(SEM["diagonals_done"], 1)
                    if n + 1 < len(ts):
                        act.wait_ge(*at("peer centred", l, ts[n + 1]))
                        done(act.activation(TOP, TOP, ACT.Exp), "peer exp", l, ts[n + 1])
                    stats(l, "fin", [t], SQ2, KB)

        @block.gpsimd
        def _(pool):
            done = Steps(pool, SEM["pool_steps"], marks, True)

            def rsqrt(ap, *name):
                pool.wait_ge(*at("plus eps", *name))
                done(pool.tensor_tensor(ap, ap, cf(K_HALF, 1).broadcast_to([P, ap.shape[-1]]), ALU.pow), "rsqrt", *name)

            for l in range(DEPTH):
                ts = tiles(l)
                for t in range(NT):
                    rsqrt(ST[:, 16 + t:17 + t], "ln1", l, t)
                for i in range(NT):
                    for d in range(2):
                        q = rsets[d]
                        if i == 0:
                            pool.wait_ge(*at("rwkv conv", l))
                        else:
                            pool.wait_ge(*at("rwkv out", l, i - 1, d))
                        done(pool.tensor_copy(split(q["T"], 4), rep(ident, 4)))
                        done(pool.tensor_copy(split(q["G"], 4), rep(ident, 4)), "rwkv TG", l, i, d)
                rsqrt(RM[:, 24:48], "group norm", l)
                rsqrt(AST[:, 32:32 + 4 * len(ts)], "attn norm", l)
                rsqrt(HM, "hgrn norm", l)
                for what in ("mix", "ln2"):
                    for t in ts:
                        rsqrt(ST[:, 16 + t:17 + t], what, l, t)
                for n, t in enumerate(ts):
                    base = (l * NT + n) * HEADS
                    if n == 0:
                        pool.wait_ge(*at("peer projected", l, WQ - 1))
                    with pool.Fori(0, HEADS) as i:
                        pool.wait_ge(SEM["heads_placed"], i + (base + 1))
                        for g in range(GROUPS):
                            c = g % RING * GROUP
                            pool.wait_ge(SEM["expert_steps"], ((i + base) * GROUPS + g) * GSTEP)
                            pool.wait_ge(SEM["experts_added"], (i + base) * GROUPS + g)
                            pool.tensor_copy(IDS[:, c:c + GROUP], IDX[n % 2][:, bass.ds(i * TOPK + g * GROUP, GROUP)])\
                                .then_inc(SEM["ids_staged"], 1)
                            pool.wait_ge(SEM["ids_staged"], (i + base) * GROUPS + (g + 1))
                            pool.tensor_tensor(DUM, ident[:, 0:1], ident[:, 0:1], ALU.mult)
                            for s in range(c, c + GROUP):
                                pool.indirect_dma_start(GB[s], None, a["uv"], IndirectOffsetOnAxis(ap=IDS[:, s:s + 1], axis=0))\
                                    .then_inc(rows_in[s], 16)
                    if n:
                        rsqrt(ST[:, 15 + t:16 + t], "fin", l, t - 1)
                rsqrt(ST[:, 16 + ts[-1]:17 + ts[-1]], "fin", l, ts[-1])

        @block.vector
        def _(dve):
            done = Steps(dve, SEM["vector_steps"], marks, True)

            def tt(o, x, y, op, *name):
                done(dve.tensor_tensor(o, x, y, op), *name)

            def ts1(o, x, s, op, *name):
                done(dve.tensor_scalar(o, x, s, None, op), *name)

            def ts2(o, x, s, r, op0, op1, *name):
                done(dve.tensor_scalar(o, x, s, r, op0, op1), *name)

            def stt(o, x, s, y, op0, op1, *name):
                done(dve.scalar_tensor_tensor(out=o, in0=x, scalar=s, in1=y, op0=op0, op1=op1), *name)

            def copy(o, x, *name):
                done(dve.tensor_copy(o, x), *name)

            def zero(o, *name):
                done(dve.memset(o, 0.0), *name)

            def rsqrt(ap, scale, eps, *name):
                ts2(ap, ap, scale, eps, ALU.mult, ALU.add, "plus eps", *name)
                dve.wait_ge(*at("rsqrt", *name))

            def normed(l, what, ts, dst):
                for t in ts:
                    dve.wait_ge(*at(what + " sum", l, t))
                    ts1(ST[:, 8 + t:9 + t], ST[:, t:t + 1], -1.0 / D, ALU.mult, what + " mean", l, t)
                for t in ts:
                    dve.wait_ge(*at(what + " squares", l, t))
                    rsqrt(ST[:, 16 + t:17 + t], 1.0 / D, EPS, what, l, t)
                    ts2(dst(t), x_tile(t), ST[:, 8 + t:9 + t], ST[:, 16 + t:17 + t], ALU.add, ALU.mult, what + " normed", l, t)

            def modulated(l, what, ts, sc, sh):
                for k in range(KB):
                    dve.wait_ge(*at(what + " turned", l, k))
                    p = 1024 * (k % 3) + 256
                    for s, lo, hi in ((1, 0, CTX), (0, CTX, T)):
                        if s == 1 and ts[0]:
                            continue
                        c, h = 2 * (sc + k) + s, 2 * (sh + k) + s
                        ts2(xt(k, lo, hi), PS[:, p + lo:p + hi], MC[:, c:c + 1], MC[:, h:h + 1], ALU.mult, ALU.add,
                            what + " modulated", l, k)

            def head_norm(o, m, n, w, scratch, eps, *name):
                tt(scratch, o, o, ALU.mult)
                done(dve.tensor_reduce(m, split(scratch, n), AX.X, ALU.add))
                rsqrt(m, 1.0 / w, eps, *name)
                tt(split(o, n), split(o, n), spread(m, w), ALU.mult)

            def rwkv_prepare(l, i, part):
                d = part % 2
                t, q = orders()[d][i], rset(i, d)
                sl = lambda ap: split(ap, 2)[:, :, t * P:(t + 1) * P]
                if part < 2:
                    for b in range(2):
                        o, x = q["b"][:, b * P:(b + 1) * P], lw_[d][:, b * T + t * P:b * T + (t + 1) * P]
                        if d:
                            o, x = o[:, ::-1], x[:, ::-1]
                        done.free(dve.tensor_tensor_scan(o, cf(K_ONES), x, 0.0, ALU.mult, ALU.add))
                    dve.wait_ge(SEM["vector_steps"], done.n)
                    end = 0 if d else P - 1
                    copy(q["bt"].unsqueeze(2), split(q["b"], 2)[:, :, end:end + 1])
                    ts1(q["mc"], q["bt"], -0.5, ALU.mult)
                    tt(split(q["b"], 2), split(q["b"], 2), spread(q["mc"], P), ALU.add)
                    done.free(dve.tensor_tensor(split(q["ta"], 2), split(q["b"], 2), sl(lw_[d]), ALU.subtract),
                              "rwkv centred", l, i, d)
                else:
                    dve.wait_ge(*at("rwkv decays", l, i, d))
                    done.free(dve.tensor_tensor(split(q["ta"], 2), split(q["ta"], 2), sl(nkk), ALU.mult))
                    done.free(dve.tensor_tensor(split(q["tr"], 2), split(q["tr"], 2), sl(r_), ALU.mult))
                    done.free(dve.tensor_tensor(split(q["tb"], 2), split(q["tk"], 2), sl(bv), ALU.mult))
                    done.free(dve.tensor_tensor(split(q["tk"], 2), split(q["tk"], 2), sl(k_), ALU.mult), "rwkv scaled", l, i, d)

            def hgrn_prepare(l, i, part):
                d, what = (0, 0, 1, 1, 0, 0, 1, 1)[part], (0, 1, 0, 1, 2, 3, 2, 3)[part]
                t, q = orders()[d][i], hset(i, d)
                sl = lambda ap: split(ap, 2)[:, :, t * P:(t + 1) * P]
                if what == 0:
                    for b in range(2):
                        o, x = q["b"][:, b * P:(b + 1) * P], HZ[d][:, b * T + t * P:b * T + (t + 1) * P]
                        if d:
                            o, x = o[:, ::-1], x[:, ::-1]
                        done.free(dve.tensor_tensor_scan(o, cf(K_ONES), x, 0.0, ALU.mult, ALU.add))
                    dve.wait_ge(SEM["vector_steps"], done.n)
                    end = 0 if d else P - 1
                    copy(q["bl"].unsqueeze(2), split(q["b"], 2)[:, :, end:end + 1])
                    tt(split(q["kh"], 2), spread(q["bl"], P), split(q["b"], 2), ALU.subtract, "hgrn sums", l, i, d)
                if what == 1:
                    for lev in range(LEVELS):
                        m = 1 << lev
                        v = q["b"].rearrange("p (n m) -> p n m", m=2 * m)
                        ref = v[:, :, m - 1 + d:m + d].broadcast_to([P, P // m, 2 * m])
                        o = q["dd"][:, lev * 256:(lev + 1) * 256].rearrange("p (n m) -> p n m", m=2 * m)
                        done.free(dve.tensor_tensor(o, v, ref, ALU.subtract), "hgrn differences", l, i, d)
                if what == 2:
                    dve.wait_ge(*at("hgrn decays", l, i, d))
                    done.free(dve.tensor_tensor(split(q["qh"], 2), split(q["eb"], 2), sl(HQ), ALU.mult))
                    done.free(dve.tensor_tensor(split(q["kh"], 2), split(q["kh"], 2), sl(HK[d]), ALU.mult), "hgrn scaled", l, i, d)
                    dve.wait_ge(*at("hgrn level decays", l, i, d))
                if what >= 2:
                    for lev in (range(3) if what == 2 else range(3, LEVELS)):
                        f = split(q["dd"][:, lev * 256:(lev + 1) * 256], 2)
                        for src, half in ((HQ, 1 - d), (HK[d], d)):
                            done.free(dve.tensor_tensor(block_runs(f, lev, half), block_runs(f, lev, half),
                                                        block_runs(sl(src), lev, half), ALU.mult), "hgrn pairs", l, i, d)

            def route(l, n, h, part):
                t = tiles(l)[n]
                first = (h + (l * NT + n) * HEADS) * ROUTING
                start = (0, 5, 7, 10, 14, 17, 22, 25, ROUTING)
                made = [start[part]]

                def step(ins):
                    made[0] += 1
                    ins.then_inc(SEM["routing_steps"], 1)
                    dve.wait_ge(SEM["routing_steps"], first + made[0])

                def search(ins, *args):
                    dve.tensor_tensor(DUM_DVE, ident[:, 0:1], ident[:, 0:1], ALU.mult)
                    step(ins(*args))

                half = part // 2
                s, values, places = CAND[:, half % 2 * P:half % 2 * P + P], SV[:, half % 2 * 16:], SI[:, half % 2 * 16:]
                if part == 0:
                    for j in range(2):
                        step(dve.tensor_copy(CAND[:, j * P:(j + 1) * P], QT[:, bass.ds(h * (2 * T) + (j * T + t * P), P)]))
                if part in (0, 2):
                    search(dve.max, values[:, 0:8], s)
                    search(dve.max_index, places[:, 0:8], values[:, 0:8], s)
                    search(dve.match_replace, s, values[:, 0:8], s, -3.0e38)
                if part in (1, 3):
                    search(dve.max, values[:, 8:16], s)
                    search(dve.max_index, places[:, 8:16], values[:, 8:16], s)
                if part == 3:
                    step(dve.tensor_copy(SIF, SI))
                    step(dve.tensor_tensor(CAND.rearrange("p (i j) -> p i j", i=16), spread(SV[:, 0:16], 16),
                                           rep(SV[:, 16:32], 16), ALU.add))
                if part == 4:
                    search(dve.max, TOP1[:, 0:8], CAND)
                    search(dve.max_index, CI[:, 0:8], TOP1[:, 0:8], CAND)
                    search(dve.match_replace, CAND, TOP1[:, 0:8], CAND, -3.0e38)
                if part == 5:
                    search(dve.max, TOP1[:, 8:16], CAND)
                    search(dve.max_index, CI[:, 8:16], TOP1[:, 8:16], CAND)
                    step(dve.tensor_single_scalar(CIJ[:, 0:16], CI, 4, ALU.logical_shift_right))
                    step(dve.tensor_single_scalar(CIJ[:, 16:32], CI, 15, ALU.bitwise_and))
                    step(dve.tensor_copy(CIJF, CIJ))
                if part == 6:
                    step(dve.tensor_tensor(split(OH, 32), spread(CIJF, 16), rep(cf(K_IOTA, 16), 32), ALU.is_equal))
                    for j in range(2):
                        o = split(OH[:, j * 256:(j + 1) * 256], 16)
                        step(dve.tensor_tensor(o, o, rep(SIF[:, j * 16:j * 16 + 16], 16), ALU.mult))
                if part == 7:
                    step(dve.tensor_reduce(E0, split(OH, 32), AX.X, ALU.add))
                    step(dve.scalar_tensor_tensor(out=E0[:, 0:16], in0=E0[:, 0:16], scalar=float(NKEYS), in1=E0[:, 16:32],
                                                  op0=ALU.mult, op1=ALU.add))
                    step(dve.tensor_scalar(E0[:, 0:16], E0[:, 0:16], float(l * EXPERTS), None, ALU.add))
                    step(dve.tensor_copy(TOP[:, bass.ds(h * 16, 16)], TOP1))
                    dve.tensor_copy(IDX[n % 2][:, bass.ds(h * 16, 16)], E0[:, 0:16]).then_inc(SEM["heads_placed"], 1)
                assert made[0] == start[part + 1]

            def centre(l, n):
                t = tiles(l)[n]
                copy(GS[:, HEADS:].unsqueeze(2), split(TOP, HEADS)[:, :, 0:1])
                tt(split(TOP, HEADS), split(TOP, HEADS), spread(GS[:, HEADS:], 16), ALU.subtract, "peer centred", l, t)

            def weigh(l, n):
                t = tiles(l)[n]
                dve.wait_ge(*at("peer exp", l, t))
                done(dve.tensor_reduce(GS[:, 0:HEADS], split(TOP, HEADS), AX.X, ALU.add))
                done(dve.reciprocal(GS[:, 0:HEADS], GS[:, 0:HEADS]))
                tt(split(GATE[n % 2], HEADS), split(TOP, HEADS), spread(GS[:, 0:HEADS], 16), ALU.mult, "routed", l, t)

            def final_norm(l, t):
                dve.wait_ge(*at("rsqrt", "fin", l, t))
                ts2(x_tile(t), x_tile(t), ST[:, 8 + t:9 + t], ST[:, 16 + t:17 + t], ALU.add, ALU.mult)
                dve.wait_ge(SEM["ln_rows_loaded"], 64 * l + 64)
                tt(split(x_tile(t), KB), split(x_tile(t), KB), LNR2[0], ALU.mult)
                tt(split(x_tile(t), KB), split(x_tile(t), KB), LNR2[1], ALU.add, "final", l, t)

            def mean_square(l, t):
                dve.wait_ge(*at("fin squares", l, t))
                ts2(ST[:, 16 + t:17 + t], ST[:, 16 + t:17 + t], 1.0 / D, EPS, ALU.mult, ALU.add, "plus eps", "fin", l, t)

            dve.wait_ge(*at("cond sigmoid"))
            tt(CC[:], CC[:], ST[:, 32:48], ALU.mult, "cond silu")
            for l in range(DEPTH):
                ts = tiles(l)
                normed(l, "ln1", range(NT), lambda t: XN[:, t * D:(t + 1) * D])
                dve.wait_ge(*at("params", l))
                LV = ROW[:, R_LAM:R_LAM + 256]
                for n in range(2):
                    done(dve.tensor_tensor_reduce(out=LV[:, n * 128:n * 128 + 64], in0=LV[:, n * 128:n * 128 + 64],
                                                  in1=LV[:, n * 128 + 64:n * 128 + 128], scale=1.0, scalar=0.0,
                                                  op0=ALU.mult, op1=ALU.add, accum_out=LAM[:, n:n + 1]), "lambda sums", l)
                dve.wait_ge(*at("lambda exp", l))
                tt(LAM[:, 2:3], LAM[:, 1:2], LAM[:, 0:1], ALU.subtract)
                lam_init = 0.8 - 0.6 * math.exp(-0.3 * l)
                ts1(LAM[:, 2:3], LAM[:, 2:3], -lam_init, ALU.add)
                if l == 0:
                    tt(LB[:, 8:10], LB[:, 0:2], LB[:, 2:4], ALU.max)
                    tt(LB[:, 4:6], LB[:, 0:2], LB[:, 8:10], ALU.subtract)
                    tt(LB[:, 6:8], LB[:, 2:4], LB[:, 8:10], ALU.subtract, "bounds shifted")
                    dve.wait_ge(*at("bounds exp"))
                    tt(LB[:, 8:10], LB[:, 4:6], LB[:, 6:8], ALU.add)
                    done(dve.reciprocal(LB[:, 8:10], LB[:, 8:10]))
                    tt(LB[:, 4:6], LB[:, 4:6], LB[:, 8:10], ALU.mult)
                    tt(LB[:, 6:8], LB[:, 6:8], LB[:, 8:10], ALU.mult)
                    tt(LB[:, 6:8], LB[:, 6:8], LB[:, 4:6], ALU.add)
                    tt(LB[:, 8:10], LB[:, 4:6], LB[:, 4:6], ALU.subtract)
                    tt(LB[:, 10:12], LB[:, 6:8], LB[:, 4:6], ALU.subtract)
                    ts2(LB[:, 12:16], LB[:, 8:12], -1.0, 1.0, ALU.mult, ALU.add)
                dve.wait_ge(*at("ada turned", l, ADA // 4 - 1))
                tt(MC[:].rearrange("p (n s) -> p n s", s=2), bank(6, 0, 96).rearrange("p (n s) -> p n s", s=2),
                   spread(COL[:, C_ADAB:C_ADAB + ADA], 2), ALU.add)
                for c in (8, 32):
                    ts1(MC[:, 2 * c:2 * c + 16], MC[:, 2 * c:2 * c + 16], 1.0, ALU.add, "mod cols", l)
                modulated(l, "ln1", range(NT), 8, 0)
                for c in range(6):
                    dve.wait_ge(*at("rwkv copied", l, c))
                    x, y = RAW[:, c * T:(c + 1) * T], CV[:, c * T:(c + 1) * T]
                    w = [COL[:, C_CONV + 6 * j + c:C_CONV + 6 * j + c + 1] for j in range(3)]
                    ts1(y, x, w[1], ALU.mult)
                    for lo, hi in ((0, CTX), (CTX, T)):
                        stt(y[:, lo + 1:hi], x[:, lo:hi - 1], w[0], y[:, lo + 1:hi], ALU.mult, ALU.add)
                        stt(y[:, lo:hi - 1], x[:, lo + 1:hi], w[2], y[:, lo:hi - 1], ALU.mult, ALU.add, "rwkv conv", l)
                blk = lambda ap, b: ap[:, b * T:(b + 1) * T]
                for b in range(2):
                    ts1(blk(nkk, b), blk(k_, b), COL[:, C_KK + b:C_KK + b + 1], ALU.mult)
                tt(bv, nkk, nkk, ALU.mult, "rwkv kk squared", l)
                for b in range(2):
                    dve.wait_ge(*at("rwkv kk norm", l, b))
                    ts1(blk(bv, b), PS[:, 1024 * b + 256:1024 * b + 1024], 1e-24, ALU.max, "rwkv kk floored", l, b)
                for b in range(2):
                    dve.wait_ge(*at("rwkv kk root", l, b))
                    done(dve.reciprocal(blk(bv, b), blk(bv, b)))
                stt(nkk, nkk, -1.0, bv, ALU.mult, ALU.mult, "rwkv kk", l)
                dve.wait_ge(*at("rwkv gate read", l, 5))
                ts2(RM[:, 0:2], COL[:, C_KA:C_KA + 2], -1.0, 1.0, ALU.mult, ALU.add)
                for b in range(2):
                    ts2(blk(bv, b), blk(RA, b), COL[:, C_KA + b:C_KA + b + 1], RM[:, b:b + 1], ALU.mult, ALU.add)
                tt(k_, k_, bv, ALU.mult)
                stt(bv, nkk, -1.0, RA, ALU.mult, ALU.mult)
                for b in range(2):
                    stt(blk(RA, b), blk(r_, b), COL[:, C_RK + b:C_RK + b + 1], blk(k_, b), ALU.mult, ALU.mult, "rwkv rk", l)
                for d in range(2):
                    ts1(lw_[d], lw_[d], -math.exp(-0.5), ALU.mult)
                dve.wait_ge(*at("rwkv bonus", l))
                copy(BON, bank(7, 0, 24))
                for d in range(2):
                    zero(rsets[d]["s"])
                    for n in ("abT", "akT", "qbT", "qkT"):
                        zero(rsets[d][n])
                dve.wait_ge(*at("rwkv v turned", l))
                zero(RO, "rwkv ready", l)
                for part in range(4):
                    rwkv_prepare(l, 0, part)
                for i in range(NT):
                    R = [(d, orders()[d][i], rset(i, d), 4 * d) for d in range(2)]
                    for d, t, q, b0 in R:
                        tt(split(q["sm"], 2), split(q["s"], 2), spread(q["em"], P), ALU.mult, "rwkv state scaled", l, i, d)
                    for d, t, q, b0 in R:
                        for n, (buf, m) in enumerate((("abT", B_STRICT), ("akT", B_STRICT), ("qbT", B_INCL), ("qkT", B_INCL))):
                            dve.wait_ge(*at("rwkv scores", l, i, d, n // 2 * 2 + 1))
                            done.free(dve.copy_predicated(parity_heads(q[buf]), rep4(mask(m + d)),
                                                          parity_banks(b0 + n // 2 * 2, n % 2 * 256)), "rwkv scores kept", l, i, d)
                    for lev in range(LEVELS):
                        for d, t, q, b0 in R:
                            dve.wait_ge(*at("rwkv AT", l, i, d, lev))
                            inv = cf(K_INV + (d * LEVELS + lev) * P)
                            if lev == 0:
                                done.free(dve.tensor_tensor(parity_heads(q["X"]), parity_banks(b0, 0), rep4(inv), ALU.mult),
                                          "rwkv X", l, i, d, lev)
                            else:
                                done.free(dve.tensor_tensor(split(q["X"], 4), split(bank(b0), 4), rep(inv, 4), ALU.mult),
                                          "rwkv X", l, i, d, lev)
                        for d, t, q, b0 in R:
                            left, right = (0, 1) if d == 0 else (1, 0)
                            if lev == 0:
                                dve.wait_ge(*at("rwkv TG", l, i, d))
                                dve.wait_ge(*at("rwkv X", l, i, d, lev))
                                v = runs(q["T"], lev, left)
                                done.free(dve.tensor_tensor(v, v, runs(q["X"], lev, left), ALU.add), "rwkv T", l, i, d, lev)
                            dve.wait_ge(*at("rwkv dT", l, i, d, lev))
                            if 0 < lev < LEVELS - 1:
                                v = runs(q["T"], lev, left)
                                done.free(dve.tensor_tensor(v, v, runs(bank(b0 + 1), lev, left), ALU.add), "rwkv T", l, i, d, lev)
                            v = runs(q["G"], lev, right)
                            done.free(dve.tensor_tensor(v, v, runs(bank(b0 + 2), lev, right), ALU.add), "rwkv G", l, i, d, lev)
                        if lev < 4 and i + 1 < NT:
                            rwkv_prepare(l, i + 1, lev)
                    for d, t, q, b0 in R:
                        dve.wait_ge(*at("rwkv out", l, i, d))
                        tt(split(q["x2"], 2), split(bank(b0 + 3, 256, 512), 2), rep(cf(K_BD), 2), ALU.mult)
                        tt(q["x2"], q["x2"], q["sm"], ALU.add)
                        tt(split(q["s"], 2), split(q["x2"], 2), spread(q["em"], P), ALU.mult)
                        o = RO[:, t * 256:(t + 1) * 256]
                        tt(o, o, bank(b0 + 2, 0, 256), ALU.add, "rwkv state", l, i, d)
                done(dve.tensor_reduce(RM[:, 0:24], split(RO, 24), AX.X, ALU.add))
                ts1(RM[:, 0:24], RM[:, 0:24], 1.0 / HD, ALU.mult)
                tt(split(RO, 24), split(RO, 24), spread(RM[:, 0:24], HD), ALU.subtract)
                head_norm(RO, RM[:, 24:48], 24, HD, RA, GN_EPS, "group norm", l)
                tt(split(RO, NT), split(RO, NT), rep(ROW[:, R_GNW:R_GNW + 256], NT), ALU.mult)
                tt(split(RO, NT), split(RO, NT), rep(ROW[:, R_GNB:R_GNB + 256], NT), ALU.add)
                tt(split(RA, 24), split(VTM, 24), spread(BON, HD), ALU.mult)
                tt(RO, RO, RA, ALU.add)
                dve.wait_ge(*at("rwkv g", l))
                tt(RO, RO, PS[:, 0:NT * 256], ALU.mult, "rwkv y", l)
                for n in range(8):
                    dve.wait_ge(*at("rotated", l, n))
                    if n == 0:
                        dve.wait_ge(*at("attn copied", l, AQK - 1))
                    x = (QA if n < 4 else KA)[:, (n % 4) * T + CTX:(n % 4 + 1) * T]
                    tt(RT, bank(6 + n % 2), cf(K_SIN, SEQ), ALU.mult)
                    tt(x, x, cf(K_COS, SEQ), ALU.mult)
                    tt(x, x, RT, ALU.add, "rope", l, n)
                jobs = [(t, h) for t in ts for h in range(BH)]
                for n in range(len(jobs) + 2):
                    if 1 <= n <= len(jobs):
                        j = n - 1
                        keys = T if jobs[j][0] >= CT else CTX
                        c0 = 16 * (j % 2)
                        p0, p1 = (PA[j % 2][m][:, 0:keys] for m in range(2))
                        dve.wait_ge(*at("attn exp", l, j, 1))
                        done(dve.reciprocal(AST[:, c0 + 6:c0 + 8], AST[:, c0 + 4:c0 + 6]))
                        tt(AST[:, c0 + 8:c0 + 9], AST[:, c0 + 7:c0 + 8], LAM[:, 2:3], ALU.mult)
                        ts1(p0, p0, AST[:, c0 + 6:c0 + 7], ALU.mult)
                        stt(p0, p1, AST[:, c0 + 8:c0 + 9], p0, ALU.mult, ALU.add, "attn a", l, j)
                    if n < len(jobs):
                        keys = T if jobs[n][0] >= CT else CTX
                        c0 = 16 * (n % 2)
                        for m in range(2):
                            dve.wait_ge(*at("attn scores", l, n, m))
                            done(dve.tensor_reduce(AST[:, c0 + m:c0 + m + 1], PS[:, 1024 * m + 256:1024 * m + 256 + keys],
                                                   AX.X, ALU.max))
                            ts1(AST[:, c0 + 2 + m:c0 + 3 + m], AST[:, c0 + m:c0 + m + 1], -SCALE, ALU.mult, "attn max", l, n, m)
                    if n >= 2:
                        j = n - 2
                        t, h = jobs[j]
                        dve.wait_ge(*at("attn pv", l, j))
                        copy(OA[:, t * 512 + h * P:t * 512 + (h + 1) * P], bank(6, 0, P), "attn o", l, j)
                n0, nt = ts[0], len(ts)
                head_norm(OA[:, n0 * 512:], AST[:, 32:32 + 4 * nt], 4 * nt, P, OS[:, 0:nt * 512], EPS, "attn norm", l)
                o = split(OA[:, n0 * 512:], 4 * nt)
                tt(o, o, rep(ROW[:, R_SUB:R_SUB + P], 4 * nt), ALU.mult)
                ts1(OA[:, n0 * 512:], OA[:, n0 * 512:], 1.0 - lam_init, ALU.mult, "attn y", l)
                dve.wait_ge(*at("hgrn q gate", l))
                tt(HQ, HQ, HS, ALU.mult)
                big = float(2.0 ** LN_SHIFT)
                for d in range(2):
                    dve.wait_ge(*at("hgrn gates", l, d))
                    for b in range(2):
                        lb, om = LB[:, 8 + 2 * l + b:9 + 2 * l + b], LB[:, 12 + 2 * l + b:13 + 2 * l + b]
                        ts2(blk(HZ[d], b), blk(HZ[d], b), om, lb, ALU.mult, ALU.add)
                        ts1(blk(HK[d], b), blk(HK[d], b), om, ALU.mult)
                    ts1(HZ[d], HZ[d], MIN_FORGET, ALU.max)
                    ts2((HO, HS)[d], HZ[d], 1.0 / big, big - 1.0, ALU.is_lt, ALU.mult)
                    stt(HZ[d], (HO, HS)[d], 1.0, HZ[d], ALU.add, ALU.mult, "hgrn f", l, d)
                for d in range(2):
                    dve.wait_ge(*at("hgrn log", l, d))
                    stt(HZ[d], (HO, HS)[d], -LN_SHIFT * math.log(2.0) / big, HZ[d], ALU.mult, ALU.add)
                    zero(hsets[d]["s"])
                    zero(hsets[d]["at"])
                zero(HO, "hgrn ready", l)
                for part in range(8):
                    hgrn_prepare(l, 0, part)
                for i in range(NT):
                    R = [(d, orders()[d][i], hset(i, d), 4 * d) for d in range(2)]
                    for n in range(LEVELS + 1):
                        for d, t, q, b0 in R:
                            dve.wait_ge(*at("hgrn level", l, i, d, n))
                            if n:
                                dve.wait_ge(*at("hgrn placed", l, i, d, n - 1))
                            src = parity_banks(b0 + 2 * (n % 2), 256)
                            if n == 0:
                                done.free(dve.copy_predicated(parity_heads(q["at"]), rep4(mask(B_DIAG)), src),
                                          "hgrn placed", l, i, d, n)
                            else:
                                lev = n - 1
                                mk = runs(mask(B_LEV + d * LEVELS + lev), lev, 1 - d)
                                for par in range(2):
                                    dst = block_runs(parity_heads(q["at"])[:, par, :, :], lev, 1 - d)
                                    done.free(dve.copy_predicated(dst, mk.unsqueeze(1).broadcast_to([P, 2, *mk.shape[1:]]),
                                                                  block_runs(src[:, par, :, :], lev, 1 - d)),
                                              "hgrn placed", l, i, d, n)
                        if i + 1 < NT:
                            hgrn_prepare(l, i + 1, n)
                    for d, t, q, b0 in R:
                        dve.wait_ge(*at("hgrn out", l, i, d))
                        done.free(dve.tensor_tensor(split(q["s1"], 2), split(bank(b0 + 2, 0, 256), 2), rep(cf(K_BD), 2), ALU.mult))
                        tt(split(q["s"], 2), split(q["s"], 2), spread(q["el"], P), ALU.mult)
                        o = HO[:, t * 256:(t + 1) * 256]
                        done.free(dve.tensor_tensor(o, o, bank(b0 + 1, 0, 256), ALU.add))
                        done.free(dve.tensor_tensor(q["s"], q["s"], q["s1"], ALU.add), "hgrn state", l, i, d)
                for d in range(2):
                    dve.wait_ge(*at("hgrn state", l, NT - 1, d))
                head_norm(HO, HM, 24, HD, HK[0], EPS, "hgrn norm", l)
                tt(split(HO, 24), split(HO, 24), rep(ROW[:, R_HN:R_HN + HD], 24), ALU.mult)
                dve.wait_ge(*at("hgrn g gate", l))
                tt(HG, HG, HS, ALU.mult)
                tt(HO, HO, HG, ALU.mult, "hgrn y", l)
                dve.wait_ge(*at("gate1 kept", l, 1 if l + 1 < DEPTH else 0))
                for half in range(2):
                    dve.wait_ge(*at("out projected", l, half))
                    for n, t in enumerate(ts):
                        c = slice(half * 512, half * 512 + 512)
                        y = XN[:, t * D:(t + 1) * D][:, c]
                        tt(y, bank(n), BC[1 if t < CT else 0][:, c], ALU.mult)
                        stt(x_tile(t)[:, c], x_tile(t)[:, c], ALPHA, y, ALU.mult, ALU.add, "mixed", l, half)
                        marks[("mix input", l, t)] = marks[("mixed", l, half)]
                normed(l, "mix", ts, lambda t: XN[:, t * D:(t + 1) * D])
                dve.wait_ge(SEM["ln_rows_loaded"], 64 * l + 32)
                for t in ts:
                    xn = XN[:, t * D:(t + 1) * D]
                    tt(xn, xn, LNR[0], ALU.mult)
                    tt(x_tile(t), xn, LNR[1], ALU.add, "ln2 input", l, t)
                normed(l, "ln2", ts, lambda t: XN[:, t * D:(t + 1) * D])
                dve.wait_ge(*at("mod2 kept", l, 1 if l + 1 < DEPTH else 0))
                dve.wait_ge(*at("out projected", l, 1))
                for t in ts:
                    s = 1 if t < CT else 0
                    u = U2[:, t * D:(t + 1) * D]
                    tt(u, XN[:, t * D:(t + 1) * D], BC[2 * s + 1], ALU.mult)
                    tt(u, u, BC[2 * s], ALU.add)
                modulated(l, "ln2", ts, 32, 24)
                marks[("peer input", l)] = marks[("ln2 modulated", l, KB - 1)]
                step = SEM["expert_steps"]
                if l == 0:
                    dve.sem_inc(step, (RING - 1) * GSTEP)
                with dve.Fori(0, HEADS) as h:
                    dve.wait_ge(SEM["first_scores_kept"], h + (l * HEADS + 1))
                    for part in range(8):
                        route(l, 0, h, part)
                centre(l, 0)
                weigh(l, 0)
                for n, t in enumerate(ts):
                    base = (l * NT + n) * HEADS
                    zero(ACC)
                    u = U2[:, t * D:(t + 1) * D]
                    if n + 1 < len(ts):
                        dve.wait_ge(*at("peer scores kept", l, ts[n + 1]))
                    with dve.Fori(0, HEADS) as i:
                        for g in range(GROUPS):
                            c = g % RING * GROUP
                            now = ((i + base) * GROUPS + (g + RING - 1)) * GSTEP
                            for s in range(c, c + GROUP):
                                dve.wait_ge(rows_in[s], ((i + base) * (GROUPS // RING) + (g // RING + 1)) * 16)
                                dve.tensor_tensor_reduce(out=GB[s][:, 0:D], in0=GB[s][:, 0:D], in1=u, scale=1.0, scalar=0.0,
                                                         op0=ALU.mult, op1=ALU.add, accum_out=DOT[:, s:s + 1]).then_inc(step, 1)
                            if n + 1 < len(ts):
                                route(l, n + 1, i, g)
                            dve.wait_ge(SEM["gelu_done"], (i + base) * GROUPS + (g + 1))
                            dve.tensor_tensor(WGT[:, c:c + GROUP], GEL[:, c:c + GROUP],
                                              GATE[n % 2][:, bass.ds(i * TOPK + g * GROUP, GROUP)], ALU.mult).then_inc(step, 1)
                            dve.wait_ge(step, now + (GROUP + 1))
                            dve.scalar_tensor_tensor(out=ACC, in0=GB[c][:, D:2 * D], scalar=WGT[:, c:c + 1], in1=ACC,
                                                     op0=ALU.mult, op1=ALU.add).then_inc(step, 1)
                    if n + 1 < len(ts):
                        dve.wait_ge(SEM["heads_placed"], base + 2 * HEADS)
                        centre(l, n + 1)
                    dve.wait_ge(step, ((base + HEADS) * GROUPS + RING - 1) * GSTEP)
                    if n == 0:
                        dve.wait_ge(*at("gate2 rows", l))
                    dve.wait_ge(SEM["experts_added"], (base + HEADS) * GROUPS + RING - 1)
                    copy(MIX, split(ACC, KB))
                    tt(MIX, MIX, split(ACC_PE, KB), ALU.add, "sums taken", l, t)
                    tt(MIX, MIX, split(gate2_row(1 if t < CT else 0), KB), ALU.mult)
                    stt(split(x_tile(t), KB), split(x_tile(t), KB), ALPHA, MIX, ALU.mult, ALU.add, "fin input", l, t)
                    if n + 1 < len(ts):
                        weigh(l, n + 1)
                    dve.wait_ge(*at("fin sum", l, t))
                    ts1(ST[:, 8 + t:9 + t], ST[:, t:t + 1], -1.0 / D, ALU.mult, "fin mean", l, t)
                    if n:
                        final_norm(l, ts[n - 1])
                    mean_square(l, t)
                final_norm(l, ts[-1])


def constants():
    f = np.zeros((P, NCF), np.float32)
    p = np.arange(P)
    f[:, K_ID:K_ID + P] = np.eye(P)
    for d in range(P):
        s = d + 16 if d % 32 < 16 else d - 16
        f[s, K_ROT + d] = -1.0 if d % 32 < 16 else 1.0
    f[:, K_ONES:K_ONES + P] = 1.0
    f[:, K_BD:K_BD + P] = (p[:, None] // 64 == p[None, :] // 64)
    n = np.arange(SEQ)
    inv = (10000.0 ** (-2.0 * np.arange(16, dtype=np.float32) / 32.0)).astype(np.float32)
    row, col = (n // GRID_W).astype(np.float32), (n % GRID_W).astype(np.float32)
    ang = np.where((p[:, None] % 64 < 32), row[None, :], col[None, :]).astype(np.float32) * inv[p % 16][:, None]
    f[:, K_COS:K_COS + SEQ] = np.cos(ang)
    f[:, K_SIN:K_SIN + SEQ] = np.sin(ang)
    f[:, K_IOTA:K_IOTA + 16] = np.arange(16)
    f[:, K_HSEL:K_HSEL + 2] = (p[:, None] // 64 == np.arange(2)[None, :])
    f[:, K_HALF] = -0.5
    b = np.zeros((P, NCB, P), np.uint8)
    s, t = p[:, None], p[None, :]
    for lev in range(LEVELS):
        same = ((s ^ t) >> lev) == 1
        b[:, B_LEV + lev] = same & (s < t)
        b[:, B_LEV + LEVELS + lev] = same & (s > t)
        f[:, K_INV + lev * P:K_INV + (lev + 1) * P] = same & (s > t)
        f[:, K_INV + (LEVELS + lev) * P:K_INV + (LEVELS + lev + 1) * P] = same & (s < t)
    b[:, B_DIAG] = s == t
    b[:, B_STRICT], b[:, B_STRICT + 1] = s < t, s > t
    b[:, B_INCL], b[:, B_INCL + 1] = s <= t, s >= t
    return f, b.reshape(P, NCB * P).view(np.uint32)


def feature_pieces(w):
    return w.reshape(KB, P, -1, P).transpose(2, 1, 0, 3).reshape(-1, P, PIECE)


def token_pieces(w):
    return w.reshape(KB // 2, 2, P, 512).transpose(0, 2, 1, 3).reshape(-1, P, PIECE)


def kernel(**inputs):
    import concourse.bacc as bacc
    from concourse.bass_utils import run_bass_kernel_spmd

    g = {k: np.asarray(v) for k, v in inputs.items()}
    pieces, cols, rows, sw, ln = [], [], [], [], []

    def column(v):
        return v.reshape(-1, P).T

    for l in range(DEPTH):
        w = g["w_in"][l]
        wo = g["w_out"][l]
        pieces += [token_pieces(g["ada_w"][l][:, c:c + 512]) for c in range(0, 6 * D, 512)]
        pieces += [feature_pieces(w[:, 0:1920][:, 0:896]),
                   feature_pieces(w[:, 896:1920]), token_pieces(w[:, 1920:2432]), feature_pieces(w[:, 2432:3200]),
                   token_pieces(w[:, 3200:3712]), token_pieces(wo[:, 0:512]), token_pieces(wo[:, 512:1024]),
                   feature_pieces(g["peer_wq"][l])]
        cols.append(np.concatenate(
            [column(g["rwkv_conv"][l, j]) for j in range(3)] + [column(g["rwkv_a0"][l])]
            + [column(g["rwkv_w0"][l, d]) for d in range(2)]
            + [column(g[n][l]) for n in ("rwkv_k_k", "rwkv_k_a", "rwkv_r_k", "ada_b")], axis=1))
        rows.append(np.concatenate([g["rwkv_ln_w"][l], g["rwkv_ln_b"][l], g["diff_subln_w"][l], g["hgrn_norm_w"][l],
                                    g["diff_lambda"][l].reshape(-1)]))
        s = np.zeros((P, 512), np.float32)
        s[0:32, 0:256], s[0:32, 256:512] = g["rwkv_w2"][l, 0], g["rwkv_w2"][l, 1]
        s[32:64, 0:256], s[64:128, 0:256] = g["rwkv_a2"][l], g["rwkv_g2"][l]
        sw.append(s)
        ln.append(np.stack([g["ln1_w"][l], g["ln1_b"][l], g["ln2_w"][l], g["ln2_b"][l]]))
    cf, cb = constants()
    arrays = {
        "x": g["x"], "ctx": g["ctx"],
        "cc": np.stack([column(g["c"][0]), column(g["c_ctx"])], axis=2).reshape(P, 2 * KB),
        "cf": cf, "cb": cb, "ws": np.concatenate(pieces), "cols": np.stack(cols), "rows": np.stack(rows),
        "sw": np.stack(sw), "ln": np.stack(ln),
        "sk": g["peer_subkeys"].transpose(0, 3, 1, 2).reshape(DEPTH, P, 2 * NKEYS),
        "lb": np.concatenate([column(g["hgrn_lb_logits"][l]) for l in range(DEPTH)], axis=1),
        "uv": np.concatenate([g["peer_u"], g["peer_v"]], axis=2).reshape(DEPTH * EXPERTS, 2 * D),
    }
    arrays = {k: np.ascontiguousarray(v) for k, v in arrays.items()}
    marks = {}
    for last in range(2):
        nc = bacc.Bacc("TRN2", target_bir_lowering=False, num_devices=1)
        args = {k: nc.dram_tensor(f"in_{k}", v.shape, mybir.dt.from_np(v.dtype), kind="ExternalInput").ap()
                for k, v in arrays.items()}
        args["out"] = nc.dram_tensor("out_x", (1, SEQ, D), F32, kind="ExternalOutput").ap()
        if last:
            marks["real"] = True
        build(nc, args, marks)
    r = run_bass_kernel_spmd(nc, [{f"in_{k}": v for k, v in arrays.items()}], core_ids=[0])
    return r.results[0]["out_x"]
```
